# Optimizing a Trainium2 kernel written in Bass

```python
import math
import jax, jax.numpy as jnp
from jax import lax
import numpy as np

D_MODEL = 1024
BATCH = 1
SEQ = 256
DEPTH = 2

GRID_W = 64
CTX_LEN = 256
MLA_HEADS = 8
QK_NOPE = 64
QK_ROPE = 32
V_HEAD = 64
Q_LORA = 384
KV_LORA = 256
CONV_CH = 256
CONV_WIDTH = 31
SC_CH = 256
SC_WIDTH = 3
N_BRANCH = 3
D_FF = int(math.ceil(8 * D_MODEL / 3 / 256)) * 256
N_MOD = 6
ROPE_THETA = 10000.0
EPS = 1e-6
Q_BLOCK = 128

Q_A_END = Q_LORA
KV_A_END = Q_A_END + KV_LORA + QK_ROPE
GLU_END = KV_A_END + 2 * CONV_CH
SC_END = GLU_END + 3 * SC_CH
GATE_END = SC_END + N_BRANCH * D_MODEL
IN_COLS = GATE_END

kernel_name = 'hybrid_mla_conformer_shortconv_dit'

def rms_norm(x, g):
    xf = x.astype(jnp.float32)
    y = xf * lax.rsqrt(jnp.mean(xf * xf, axis=-1, keepdims=True) + EPS)
    return (y * g.astype(jnp.float32)).astype(x.dtype)

def layer_norm(x, g, b):
    xf = x.astype(jnp.float32)
    mu = jnp.mean(xf, axis=-1, keepdims=True)
    var = jnp.mean(jnp.square(xf - mu), axis=-1, keepdims=True)
    y = (xf - mu) * lax.rsqrt(var + EPS)
    return (y * g.astype(jnp.float32) + b.astype(jnp.float32)).astype(x.dtype)

def modulate(x, shift, scale):
    return x * (1 + scale) + shift

def depthwise_conv(u, w):
    k = w.shape[0]
    pad = (k - 1) // 2
    return lax.conv_general_dilated(
        u, w[:, None, :].astype(u.dtype), window_strides=(1,), padding=[(pad, pad)],
        dimension_numbers=('NWC', 'WIO', 'NWC'), feature_group_count=u.shape[-1])

def axial_rope_tables(n):
    rows = n // GRID_W
    row = jnp.repeat(jnp.arange(rows, dtype=jnp.float32), GRID_W)
    col = jnp.tile(jnp.arange(GRID_W, dtype=jnp.float32), rows)
    half = QK_ROPE // 2
    inv = jnp.power(jnp.float32(ROPE_THETA), -jnp.arange(0, half, 2, dtype=jnp.float32) / half)
    ang_r = row[:, None] * inv
    ang_c = col[:, None] * inv
    return (jnp.cos(ang_r), jnp.sin(ang_r), jnp.cos(ang_c), jnp.sin(ang_c))

def _rotate(x, cos, sin):
    x1, x2 = jnp.split(x, 2, axis=-1)
    return jnp.concatenate([x1 * cos - x2 * sin, x1 * sin + x2 * cos], axis=-1)

def apply_axial_rope(x, tables):
    extra = x.ndim - 3
    cr, sr, cc, sc = [t.reshape(t.shape[0], *([1] * extra), t.shape[1]).astype(x.dtype) for t in tables]
    xr, xc = jnp.split(x, 2, axis=-1)
    return jnp.concatenate([_rotate(xr, cr, sr), _rotate(xc, cc, sc)], axis=-1)

def mla_queries(q_a, q_norm_g, w_q_b):
    q = rms_norm(q_a, q_norm_g) @ w_q_b
    q = q.reshape(*q_a.shape[:-1], MLA_HEADS, QK_NOPE + QK_ROPE)
    return q[..., :QK_NOPE], q[..., QK_NOPE:]

def mla_keys_values(kv_a, kv_norm_g, w_kv_b):
    c_kv = rms_norm(kv_a[..., :KV_LORA], kv_norm_g)
    k_rope = kv_a[..., KV_LORA:]
    kv = (c_kv @ w_kv_b).reshape(*kv_a.shape[:-1], MLA_HEADS, QK_NOPE + V_HEAD)
    return kv[..., :QK_NOPE], k_rope, kv[..., QK_NOPE:]

def attend(q_nope, q_rope, k_nope, k_rope, v):
    scale = (QK_NOPE + QK_ROPE) ** -0.5
    s = jnp.einsum('bqhd,bkhd->bhqk', q_nope, k_nope) + jnp.einsum('bqhr,bkr->bhqk', q_rope, k_rope)
    p = jax.nn.softmax(s.astype(jnp.float32) * scale, axis=-1).astype(v.dtype)
    return jnp.einsum('bhqk,bkhd->bqhd', p, v)

def blockwise_attend(q_nope, q_rope, k_nope, k_rope, v):
    b, n = q_nope.shape[:2]
    nb = n // Q_BLOCK

    def to_blocks(t):
        return jnp.moveaxis(t.reshape(b, nb, Q_BLOCK, *t.shape[2:]), 1, 0)

    out = lax.map(lambda qs: attend(qs[0], qs[1], k_nope, k_rope, v),
                  (to_blocks(q_nope), to_blocks(q_rope)))
    return jnp.moveaxis(out, 0, 1).reshape(b, n, MLA_HEADS * V_HEAD)

def conformer_conv(glu_in, dw, dw_b, ln_g, ln_b, w_out):
    a, g = jnp.split(glu_in, 2, axis=-1)
    u = depthwise_conv(a * jax.nn.sigmoid(g), dw) + dw_b
    u = jax.nn.silu(layer_norm(u, ln_g, ln_b))
    return u @ w_out

def short_conv(sc_in, dw, w_out):
    bg, cg, xin = jnp.split(sc_in, 3, axis=-1)
    return (bg * depthwise_conv(cg * xin, dw)) @ w_out

def merge_branches(gate_in, y_att, y_conv, y_sc, w_o):
    g_att, g_conv, g_sc = jnp.split(jax.nn.sigmoid(gate_in), N_BRANCH, axis=-1)
    return (g_att * y_att + g_conv * y_conv + g_sc * y_sc) @ w_o

def swiglu(h, w1, w3, w2):
    return (jax.nn.silu(h @ w1) * (h @ w3)) @ w2

def setup_inputs(seed: int = 0) -> dict:
    key = jax.random.key(seed)
    ks = iter(jax.random.split(key, 32))

    def nrm(shape, scale):
        return jax.random.normal(next(ks), shape, jnp.float32) * scale

    def gain(shape):
        return 1.0 + nrm(shape, 0.02)

    return {
        'x': nrm((BATCH, SEQ, D_MODEL), 1.0),
        'c': nrm((BATCH, D_MODEL), 1.0),
        'ctx': nrm((BATCH, CTX_LEN, D_MODEL), 1.0),
        'c_ctx': nrm((D_MODEL,), 1.0),
        'w_mod': nrm((DEPTH, D_MODEL, N_MOD * D_MODEL), 0.5 * D_MODEL ** -0.5),
        'b_mod': nrm((DEPTH, N_MOD * D_MODEL), 0.01),
        'ln1_g': gain((DEPTH, D_MODEL)),
        'w_in': nrm((DEPTH, D_MODEL, IN_COLS), D_MODEL ** -0.5),
        'q_a_norm_g': gain((DEPTH, Q_LORA)),
        'w_q_b': nrm((DEPTH, Q_LORA, MLA_HEADS * (QK_NOPE + QK_ROPE)), Q_LORA ** -0.5),
        'kv_a_norm_g': gain((DEPTH, KV_LORA)),
        'w_kv_b': nrm((DEPTH, KV_LORA, MLA_HEADS * (QK_NOPE + V_HEAD)), KV_LORA ** -0.5),
        'w_mla_o': nrm((DEPTH, MLA_HEADS * V_HEAD, D_MODEL), (MLA_HEADS * V_HEAD) ** -0.5),
        'conv_dw': nrm((DEPTH, CONV_WIDTH, CONV_CH), CONV_WIDTH ** -0.5),
        'conv_dw_b': nrm((DEPTH, CONV_CH), 0.01),
        'conv_ln_g': gain((DEPTH, CONV_CH)),
        'conv_ln_b': nrm((DEPTH, CONV_CH), 0.01),
        'w_conv_o': nrm((DEPTH, CONV_CH, D_MODEL), CONV_CH ** -0.5),
        'sc_dw': nrm((DEPTH, SC_WIDTH, SC_CH), SC_WIDTH ** -0.5),
        'w_sc_o': nrm((DEPTH, SC_CH, D_MODEL), SC_CH ** -0.5),
        'w_o': nrm((DEPTH, D_MODEL, D_MODEL), D_MODEL ** -0.5),
        'ln2_g': gain((DEPTH, D_MODEL)),
        'w_ff1': nrm((DEPTH, D_MODEL, D_FF), D_MODEL ** -0.5),
        'w_ff3': nrm((DEPTH, D_MODEL, D_FF), D_MODEL ** -0.5),
        'w_ff2': nrm((DEPTH, D_FF, D_MODEL), D_FF ** -0.5),
        'final_g': gain((D_MODEL,)),
    }

def reference(x, c, ctx, c_ctx, w_mod, b_mod, ln1_g, w_in, q_a_norm_g, w_q_b, kv_a_norm_g,
              w_kv_b, w_mla_o, conv_dw, conv_dw_b, conv_ln_g, conv_ln_b, w_conv_o, sc_dw, w_sc_o,
              w_o, ln2_g, w_ff1, w_ff3, w_ff2, final_g):
    b, n, _ = x.shape
    n_ctx = ctx.shape[1]
    rope = axial_rope_tables(n)
    c_act = jax.nn.silu(c)
    cc_act = jax.nn.silu(c_ctx)
    xc = ctx
    for l in range(DEPTH):
        last = l == DEPTH - 1
        sh1, sc1, g1, sh2, sc2, g2 = jnp.split((c_act @ w_mod[l] + b_mod[l])[:, None, :], N_MOD, axis=-1)
        mod_c = jnp.split(cc_act @ w_mod[l] + b_mod[l], N_MOD, axis=-1)

        hc = modulate(rms_norm(xc, ln1_g[l]), mod_c[0], mod_c[1])
        if last:
            kvc_a = hc @ w_in[l][:, Q_A_END:KV_A_END]
        else:
            projc = hc @ w_in[l]
            kvc_a = projc[..., Q_A_END:KV_A_END]
        kc_nope, kc_rope, vc = mla_keys_values(kvc_a, kv_a_norm_g[l], w_kv_b[l])
        if not last:
            qc_nope, qc_rope = mla_queries(projc[..., :Q_A_END], q_a_norm_g[l], w_q_b[l])
            att_c = attend(qc_nope, qc_rope, kc_nope, kc_rope, vc).reshape(b, n_ctx, MLA_HEADS * V_HEAD) @ w_mla_o[l]
            conv_c = conformer_conv(projc[..., KV_A_END:GLU_END], conv_dw[l], conv_dw_b[l],
                                    conv_ln_g[l], conv_ln_b[l], w_conv_o[l])
            scv_c = short_conv(projc[..., GLU_END:SC_END], sc_dw[l], w_sc_o[l])
            xc = xc + mod_c[2] * merge_branches(projc[..., SC_END:GATE_END], att_c, conv_c, scv_c, w_o[l])
            hc2 = modulate(rms_norm(xc, ln2_g[l]), mod_c[3], mod_c[4])
            xc = xc + mod_c[5] * swiglu(hc2, w_ff1[l], w_ff3[l], w_ff2[l])

        h = modulate(rms_norm(x, ln1_g[l]), sh1, sc1)
        proj = h @ w_in[l]
        q_nope, q_rope = mla_queries(proj[..., :Q_A_END], q_a_norm_g[l], w_q_b[l])
        k_nope, k_rope, v = mla_keys_values(proj[..., Q_A_END:KV_A_END], kv_a_norm_g[l], w_kv_b[l])
        q_rope = apply_axial_rope(q_rope, rope)
        k_rope = apply_axial_rope(k_rope, rope)
        att = blockwise_attend(q_nope, q_rope,
                               jnp.concatenate([k_nope, kc_nope], axis=1),
                               jnp.concatenate([k_rope, kc_rope], axis=1),
                               jnp.concatenate([v, vc], axis=1)) @ w_mla_o[l]
        y_conv = conformer_conv(proj[..., KV_A_END:GLU_END], conv_dw[l], conv_dw_b[l],
                                conv_ln_g[l], conv_ln_b[l], w_conv_o[l])
        y_sc = short_conv(proj[..., GLU_END:SC_END], sc_dw[l], w_sc_o[l])
        x = x + g1 * merge_branches(proj[..., SC_END:GATE_END], att, y_conv, y_sc, w_o[l])
        h2 = modulate(rms_norm(x, ln2_g[l]), sh2, sc2)
        x = x + g2 * swiglu(h2, w_ff1[l], w_ff3[l], w_ff2[l])
    return rms_norm(x, final_g)


_drawn_inputs = setup_inputs


def setup_inputs(seed=0):
    import zlib

    import numpy as np

    out = dict(_drawn_inputs(seed))
    spreads = {}
    factors = {'ctx': 4.631,
     'b_mod': 3.288,
     'ln1_g': 5.147,
     'q_a_norm_g': 27.337,
     'w_q_b': 2.718,
     'kv_a_norm_g': 26.359,
     'conv_dw_b': 64.0,
     'conv_ln_g': 200.0,
     'conv_ln_b': 200.0,
     'ln2_g': 21.222,
     'final_g': 23.082}
    for name, (base, spread) in spreads.items():
        noise = np.random.default_rng([zlib.crc32(name.encode()), seed]).standard_normal(out[name].shape)
        drawn = base * np.exp(spread * noise) if base else spread * noise
        out[name] = __import__('jax').numpy.asarray(drawn.astype(out[name].dtype))
    for name, factor in factors.items():
        out[name] = (out[name] * factor).astype(out[name].dtype)
    return out
```

```python
import math
from contextlib import ExitStack, contextmanager

import concourse.bass as bass
from concourse import mybir

D = 1024
SEQ = 256
DEPTH = 2
HEADS, NOPE, ROPE, VH = 8, 64, 32, 64
QL, KVL = 384, 256
CH = 256
TAPS, SC_TAPS = 31, 3
FF = 2816
GRID_W = 64
EPS = 1e-6
P = 128
DT = D // P
T = 2 * SEQ
KV0 = QL
ROPE0 = KV0 + KVL
GLU0 = ROPE0 + ROPE
SC0 = GLU0 + 2 * CH
GATE0 = SC0 + 3 * CH
SCALE = (NOPE + ROPE) ** -0.5
CW = 256
SLOT = DT * CW
NMOD = 6
MODC = NMOD * D // CW

LN1, LN2, QG, KVG, CB, LNG, LNB, CDW, SCW = 0, 8, 16, 19, 21, 23, 25, 27, 27 + 2 * TAPS
ROWS = SCW + 2 * SC_TAPS
N_VEC = 2 * 9 + 4 + 1
FING, CVEC = 0, 8
TAPS_BEFORE, TAPS_PER_PAIR = 3, 7
PAIRS = HEADS // 2
FF_GROUPS = [8, 8, 6]


class Tally:

    def __init__(self):
        self.n, self.var, self.step = 0, None, 0

    def now(self):
        return self.n if self.var is None else self.var * self.step + self.n

    def next(self):
        self.n += 1
        return self.now()


@contextmanager
def turns(eng, times, steps):
    before = [(t, t.n, k) for t, k in steps]
    with eng.Fori(0, times) as i:
        for t, _, k in before:
            t.var, t.step = i, k
        yield i
    for t, n, k in before:
        assert t.n - n == k, (t.n - n, k, steps.index((t, k)))
        t.n, t.var, t.step = n + k * times, None, 0


class Tile:

    def __init__(self, bank, done, before, drained):
        self.bank, self.done, self.before, self.drained = bank, done, before, drained


class Place:

    def __init__(self):
        self.chunk, self.tiles, self.operand, self.unit, self.square, self.heads, self.gates = (Tally() for _ in range(7))
        self.uses = [Tally() for _ in range(4)]
        self.ring = 0
        self.z = 0

    def tile(self):
        b = self.ring % 4
        self.ring += 1
        before = self.uses[b].now()
        return Tile(b, self.tiles.next(), before, self.uses[b].next())

    @contextmanager
    def loop(self, eng, times, chunks=0, tiles=0, operands=0, units=0, squares=0, heads=0, gates=0, extra=()):
        self.ring = 0
        steps = [(self.chunk, chunks), (self.tiles, tiles), (self.operand, operands),
                 (self.unit, units), (self.square, squares), (self.heads, heads), (self.gates, gates), *extra]
        steps += [(u, (tiles - b + 3) // 4 if tiles > b else 0) for b, u in enumerate(self.uses)]
        assert times > 1
        with turns(eng, times, steps) as i:
            yield i
        self.ring = 0


def build(nc, x, c, ctx_in, c_ctx, w_mod, b_mod, ln1_g, w_in, q_a_norm_g, w_q_b, kv_a_norm_g,
          w_kv_b, w_mla_o, conv_dw, conv_dw_b, conv_ln_g, conv_ln_b, w_conv_o, sc_dw, w_sc_o,
          w_o, ln2_g, w_ff1, w_ff3, w_ff2, final_g, rope, out):
    F32, F32R = mybir.dt.float32, mybir.dt.float32r
    ACT, ALU, AX = mybir.ActivationFunctionType, mybir.AluOpType, mybir.AxisListType

    stack = ExitStack()
    with stack:
        def sb(name, shape, dt=F32):
            return stack.enter_context(nc.sbuf_tensor(name, shape, dt))

        def sem(name):
            return stack.enter_context(nc.semaphore(name))

        X = sb("X", [P, DT, T])
        Wraw = sb("Wraw", [P, 2, SLOT])
        Whi = sb("Whi", [P, 2, SLOT], F32R)
        Wlo = sb("Wlo", [P, 2, SLOT], F32R)
        Hhi = sb("Hhi", [P, DT, T], F32R)
        Hlo = sb("Hlo", [P, DT, T], F32R)
        G = sb("G", [P, DT, T])
        Uhi = sb("Uhi", [P, 9, T], F32R)
        Ulo = sb("Ulo", [P, 9, T], F32R)
        QT, CT0, AT0, CO0, SO0 = 0, 3, 5, 0, 2
        Qb = sb("Qb", [96, 2, T])
        Kb = sb("Kb", [96, 2, T])
        V = sb("V", [P, 4, P])
        PR = sb("PR", [P, 2, T])
        PTs = sb("PTs", [P, 2, T])
        PAD = TAPS // 2
        U = sb("U", [P, 2, 2, SEQ + 2 * PAD])
        ACC = sb("ACC", [P, 2, T])
        C = sb("C", [P, 2, 2, SEQ + 2])
        BG = sb("BG", [P, 2, T])
        SQ = sb("SQ", [P, 2, T])
        SUM = sb("SUM", [P, T])
        ROOT = sb("ROOT", [P, T])
        RSTD = sb("RSTD", [P, T])
        Z = sb("Z", [P, 2, T])
        TG = sb("TG", [P, 2, T])
        TAB = sb("TAB", [P, T])
        IDN = sb("IDN", [P, P])
        ONES = sb("ONES", [P, P])
        PAR = sb("PAR", [P, 4, P])
        MOD = sb("MOD", [P, DEPTH, NMOD * DT, 2])
        AV = sb("AV", [P, DT, 2])
        CTH = sb("CTH", [P, 16])
        CS = sb("CS", [P, 2, DT])
        CV = sb("CV", [P, DT, 4], F32R)
        SEL = sb("SEL", [4, 2])
        ROW = PTs[0:4, :, 0:CW]
        NM = sb("NM", [P, 2])
        RS = sb("RS", [P, 2])
        RR = sb("RR", [P, 2])
        PST = TG

        banks = [stack.enter_context(nc.psum_tensor(f"bank{b}", [P, T], F32)) for b in range(4)]
        S = [stack.enter_context(nc.psum_tensor(f"scores{b}", [P, T], F32)) for b in range(2)]
        PT = stack.enter_context(nc.psum_tensor("probsT", [P, T], F32))
        PV = stack.enter_context(nc.psum_tensor("attended", [P, T], F32))

        x_in = sem("x_in")
        vec_in = sem("vec_in")
        consts = sem("consts")
        raw_in = [sem("raw_in0"), sem("raw_in1")]
        slot_free = sem("slot_free")
        hi_done = sem("hi_done")
        lo_done = [sem("lo_done0"), sem("lo_done1")]
        tile_done = sem("tile_done")
        drained = [sem(f"drained{b}") for b in range(4)]
        sq_done = sem("sq_done")
        sq_summed = sem("sq_summed")
        root_done = sem("root_done")
        z_done = sem("z_done")
        op_hi = sem("op_hi")
        op_lo = sem("op_lo")
        q_nope = sem("q_nope")
        qk_done = sem("qk_done")
        max_done = sem("max_done")
        exp_done = sem("exp_done")
        prob_done = sem("prob_done")
        turned = sem("turned")
        turned_copied = sem("turned_copied")
        pv_done = sem("pv_done")
        dve_step = sem("dve_step")
        gate_tanh = sem("gate_tanh")
        out_ready = sem("out_ready")
        pool_step = sem("pool_step")
        conv_sq = sem("conv_sq")
        conv_v = sem("conv_v")
        conv_t = sem("conv_t")
        conv_s = sem("conv_s")
        q_ready = sem("q_ready")
        cond_tanh = sem("cond_tanh")
        cond_done = sem("cond_done")
        conv_a = sem("conv_a")
        fin_z = sem("fin_z")
        stored = sem("stored")

        block = stack.enter_context(nc.Block())

        def pair_views(w, slot, packed):
            n = 2 * P if packed else 2 * (NOPE + ROPE)
            q = w[:, slot, 0:3 * n].rearrange("p (g n) -> p g n", g=6)
            kv = w[:, slot, 3 * n:3 * n + 2 * CW]
            return q, kv

        def parts(kind, slot):
            if kind == "plain":
                return [(Wraw[:, slot, :], Whi[:, slot, :], Wlo[:, slot, :])]
            if kind == "quarter":
                n = SLOT // 4
                return [(Wraw[:, slot, 0:n], Whi[:, slot, 0:n], Wlo[:, slot, 0:n])]
            res = []
            if kind == "rope":
                src = Wraw[:, slot, 0:DT * ROPE].rearrange("p (g n) -> p g n", g=DT)
                dst = [w[:, slot, 0:DT * 2 * ROPE].rearrange("p (g n) -> p g n", g=DT) for w in (Whi, Wlo)]
                at, to, cols = 0, ROPE, slice(0, ROPE)
            else:
                src, kvs = pair_views(Wraw, slot, False)
                both = [pair_views(w, slot, True) for w in (Whi, Wlo)]
                dst = [q for q, _ in both]
                for e in range(2):
                    raw = kvs.rearrange("p (k h e d) -> p k h e d", k=2, h=2, e=2)[:, :, :, e, :]
                    res.append((raw, *[kv.rearrange("p (k e h d) -> p k e h d", k=2, h=2, e=2)[:, :, e, :, :]
                                       for _, kv in both]))
                at, to, cols = NOPE, NOPE + ROPE, slice(0, NOPE + ROPE)
            res.append((src[:, :, cols], dst[0][:, :, cols], dst[1][:, :, cols]))
            for g in range(2):
                for b in range(2):
                    s0, d0 = at + 16 * g + 8 * (1 - b), to + 16 * g + 8 * b
                    res.append((src[:, :, s0:s0 + 8], dst[0][:, :, d0:d0 + 8], dst[1][:, :, d0:d0 + 8]))
            return res

        def split_hi(act, at, kind):
            slot = at.chunk.n % 2
            n = at.chunk.n
            if at.chunk.var is None:
                act.wait_ge(raw_in[slot], 32 * (n // 2 + 1))
            else:
                act.wait_ge(raw_in[slot], at.chunk.var * (16 * at.chunk.step) + 32 * (n // 2 + 1))
            if at.tiles.n:
                act.wait_ge(tile_done, at.tiles.now())
            for raw, hi, _ in parts(kind, slot):
                last = act.activation(hi, raw, ACT.Copy)
            last.then_inc(hi_done, 1)
            at.chunk.next()

        def split_lo(eng, mine, at, kind):
            slot = at.chunk.n % 2
            if slot == mine:
                eng.wait_ge(hi_done, at.chunk.now() + 1)
                for raw, hi, lo in parts(kind, slot):
                    last = eng.tensor_tensor(lo, raw, hi.bitcast(F32), ALU.subtract)
                last.then_inc(lo_done[slot], 1)
            at.chunk.next()

        NS = [2, 1]
        half = [slice(s * SEQ, (s + 1) * SEQ) for s in range(2)]

        def by_stream(ap, l):
            return ap.rearrange("p (s n) -> p s n", s=2)[:, 0:NS[l], :]

        def units_of(l):
            return [(h, s * SEQ + q * P, 2 * s, 4 - 2 * s)
                    for h in range(2) for s in range(NS[l]) for q in range(2)]

        def stat_root(l, k):
            return 5 * l + k + 1

        @block.sync
        def _(sp):
            at = Place()
            sp.dma_start(G[:, 0:4, :].rearrange("p (t h) n -> p t (h n)", t=2),
                         x[0].rearrange("(t p) d -> p t d", p=P)).then_inc(x_in, 16)
            sp.dma_start(G[:, 4:8, :].rearrange("p (t h) n -> p t (h n)", t=2),
                         ctx_in[0].rearrange("(t p) d -> p t d", p=P)).then_inc(x_in, 16)

            def load(pieces):
                slot, n = at.chunk.n % 2, at.chunk.n
                if n >= 2:
                    if at.chunk.var is None:
                        sp.wait_ge(lo_done[slot], n // 2)
                    else:
                        sp.wait_ge(lo_done[slot], at.chunk.var * (at.chunk.step // 2) + n // 2)
                        sp.sem_inc(slot_free, 1)
                for off, k, w, src in pieces:
                    sp.dma_start(Wraw[:, slot, off:off + k * w].rearrange("p (k n) -> p k n", k=k),
                                 src.rearrange("(k p) n -> p k n", p=P)).then_inc(raw_in[slot], 16)
                at.chunk.next()

            def block_of(w, row0, k, col, width):
                h = (k + 1) // 2
                return [(0, h, width, w[row0:row0 + h * P, bass.ds(col, width)]),
                        (h * width, k - h, width, w[row0 + h * P:row0 + k * P, bass.ds(col, width)])]

            def mods(l, first, n):
                for j in range(2):
                    load(block_of(w_mod[l], 0, DT, (first + j) * CW, CW))

                def more(i):
                    for j in range(2):
                        load(block_of(w_mod[l], 0, DT, i * (2 * CW) + (first + 2 + j) * CW, CW))

                if n > 4:
                    with at.loop(sp, n // 2 - 1, chunks=2) as i:
                        more(i)
                else:
                    more(0)

            mods(0, 0, 8)
            for l in range(DEPTH):
                wi = w_in[l]
                for col, width in ((KV0, CW), (ROPE0, ROPE), (0, CW), (CW, QL - CW), (GLU0 + CH, CH), (GLU0, CH),
                                   (SC0 + CH, CH), (SC0 + 2 * CH, CH), (SC0, CH)):
                    load(block_of(wi, 0, DT, col, width))
                if l == 0:
                    mods(0, 8, 8)
                wq, wkv = w_q_b[l], w_kv_b[l]

                def pair(p):
                    n = 2 * (NOPE + ROPE)
                    load([(0, 3, n, wq[:, bass.ds(p * n, n)]), (3 * n, 2, CW, wkv[:, bass.ds(p * CW, CW)])])
                    load(block_of(wi, 0, DT, p * CW + GATE0, CW))

                with at.loop(sp, PAIRS - 1, chunks=2) as i:
                    pair(i)
                pair(PAIRS - 1)
                for j in range(2):
                    load(block_of(w_mla_o[l], 0, 4, j * 512, 512))
                with at.loop(sp, 4, chunks=4) as i:
                    load(block_of(wi, 0, DT, i * CW + (GATE0 + D), CW))
                    load(block_of(w_conv_o[l], 0, 2, i * CW, CW))
                    load(block_of(wi, 0, DT, i * CW + (GATE0 + 2 * D), CW))
                    load(block_of(w_sc_o[l], 0, 2, i * CW, CW))
                if l == 0:
                    mods(0, 16, 4)
                with at.loop(sp, 2, chunks=2) as i:
                    for j in range(2):
                        load(block_of(w_o[l], 0, DT, i * (2 * CW) + j * CW, CW))
                if l == 0:
                    mods(0, 20, 4)
                g0 = 0
                for g, n in enumerate(FF_GROUPS):
                    with at.loop(sp, n // 2, chunks=2) as i:
                        load(block_of(w_ff1[l], 0, DT, i * CW + g0 * P, CW))
                        load(block_of(w_ff3[l], 0, DT, i * CW + g0 * P, CW))
                    if l == 0:
                        mods(1, 8 * g, 8)
                    with at.loop(sp, 2, chunks=2) as i:
                        for j in range(2):
                            load(block_of(w_ff2[l], g0 * P, n, i * (2 * CW) + j * CW, CW))
                    g0 += n
            for t in range(2):
                sp.wait_ge(out_ready, 2 * (t + 1))
                sp.dma_start(out[0, t * P:(t + 1) * P, :].rearrange("p (h n) -> p h n", h=2),
                             X[:, 2 * t:2 * t + 2, :]).then_inc(stored, 16)
            sp.wait_ge(stored, 32)

        @block.gpsimd
        def _(pool):
            at = Place()
            step = Tally()

            def mark(ins):
                ins.then_inc(pool_step, 1)
                return step.next()

            mark(pool.memset(IDN[:, :], 0.0))
            v = mark(pool.memset(SEL[:, :], 0.0))
            pool.memset(ONES[:, :], 1.0).then_inc(consts, 1)
            pool.wait_ge(pool_step, v)
            pool.affine_select(out=IDN[:, :], in_=IDN[:, :], compare_op=ALU.not_equal, fill=1.0,
                               base=0, pattern=[[-1, P]], channel_multiplier=1).then_inc(consts, 1)
            for base in (0, -2):
                v = mark(pool.affine_select(out=SEL[:, :], in_=SEL[:, :], compare_op=ALU.not_equal, fill=1.0,
                                            base=base, pattern=[[-1, 2]], channel_multiplier=1))
                pool.wait_ge(pool_step, v)
            pool.memset(U[:, :, :, :].rearrange("p a b c -> p (a b c)"), 0.0).then_inc(consts, 1)
            pool.memset(C[:, :, :, :].rearrange("p a b c -> p (a b c)"), 0.0).then_inc(consts, 1)

            def clear_sum(roots):
                if roots:
                    pool.wait_ge(root_done, roots)
                v = mark(pool.memset(SUM[:, :], 0.0))
                pool.wait_ge(pool_step, v)

            def add_square(n):
                slot = at.square.n % 2
                if at.square.n:
                    pool.wait_ge(sq_summed, at.square.now())
                pool.wait_ge(sq_done, at.square.now() + 1)
                pool.tensor_tensor(SUM[:, 0:n], SUM[:, 0:n], SQ[:, slot, 0:n], ALU.add).then_inc(sq_summed, 1)
                at.square.next()

            def look(kind="plain"):
                split_lo(pool, 0, at, kind)

            def mods(n, after="plain"):
                if n > 4:
                    with at.loop(pool, n // 2 - 1, chunks=2):
                        look()
                        look()
                else:
                    look()
                    look()
                look()
                look(after)

            look()
            clear_sum(0)
            for _ in range(DT):
                add_square(T)
            mods(8)
            for l in range(DEPTH):
                TQ = NS[l] * SEQ
                look("rope")
                clear_sum(stat_root(l, 0))
                add_square(T)
                add_square(T)
                look()
                look()
                look()
                clear_sum(stat_root(l, 1))
                for _ in range(3):
                    add_square(TQ)
                for _ in range(4):
                    look()
                if l == 0:
                    look()
                    mods(8, "pair")
                else:
                    look("pair")
                with at.loop(pool, PAIRS - 1, chunks=2):
                    look()
                    look("pair")
                for _ in range(4):
                    look()
                with at.loop(pool, 4, chunks=4):
                    look("quarter")
                    look()
                    look("quarter")
                    look()
                if l == 0:
                    mods(4)
                clear_sum(stat_root(l, 2))
                with at.loop(pool, 2, chunks=2, squares=4):
                    for _ in range(2):
                        look()
                        add_square(TQ)
                        add_square(TQ)
                if l == 0:
                    mods(4)
                for g, n in enumerate(FF_GROUPS):
                    last = g == len(FF_GROUPS) - 1
                    with at.loop(pool, n // 2, chunks=2):
                        look()
                        look()
                    if l == 0:
                        mods(8)
                    if last:
                        clear_sum(stat_root(l, 4))
                    if last and l == DEPTH - 1:
                        for j in range(4):
                            if j < 3:
                                look()
                            add_square(TQ)
                            add_square(TQ)
                    else:
                        with at.loop(pool, 2, chunks=2, squares=4 * last):
                            for _ in range(2):
                                look()
                                for _ in range(2 * last):
                                    add_square(TQ)

        @block.scalar
        def _(act):
            at = Place()

            def rows(block, row, src):
                n = src.shape[0]
                act.dma_start(PST[row:row + n, 0, block * P:(block + 1) * P], src).then_inc(vec_in, 16)

            for l in range(DEPTH):
                for row, v in ((LN1, ln1_g), (LN2, ln2_g), (QG, q_a_norm_g), (KVG, kv_a_norm_g),
                               (CB, conv_dw_b), (LNG, conv_ln_g), (LNB, conv_ln_b)):
                    rows(l, row, v[l].rearrange("(t p) -> t p", p=P))
                for row, v in ((CDW, conv_dw), (SCW, sc_dw)):
                    rows(l, row, v[l].rearrange("w (t p) -> (w t) p", p=P))
            rows(2, 0, b_mod.rearrange("l (t p) -> (l t) p", p=P))
            rows(3, FING, final_g.rearrange("(t p) -> t p", p=P))
            rows(3, CVEC, c[0].rearrange("(t p) -> t p", p=P))
            rows(3, CVEC + DT, c_ctx.rearrange("(t p) -> t p", p=P))
            act.dma_start(TAB[:, :], rope).then_inc(vec_in, 16)

            def look(kind="plain"):
                split_hi(act, at, kind)

            def copy_out(dst, n=T, func=ACT.Copy, scale=1.0, m=P):
                t = at.tile()
                act.wait_ge(tile_done, t.done)
                act.activation(dst, banks[t.bank][0:m, 0:n], func, scale=scale).then_inc(drained[t.bank], 1)
                return t

            def square(src, n):
                slot = at.square.n % 2
                if at.square.n >= 2:
                    act.wait_ge(sq_summed, at.square.now() - 1)
                act.activation(SQ[:, slot, 0:n], src, ACT.Square).then_inc(sq_done, 1)
                at.square.next()

            def root(n, width):
                t = at.tile()
                act.wait_ge(tile_done, t.done)
                act.activation(ROOT[:, 0:n], banks[t.bank][:, 0:n], ACT.Sqrt, bias=EPS,
                               scale=1.0 / width).then_inc(root_done, 1)

            def mods(n, after="plain"):
                def two(after):
                    look()
                    copy_out(ROW[:, 0, :], CW, m=4)
                    look(after)
                    copy_out(ROW[:, 1, :], CW, m=4)
                    at.tile()
                    at.tile()
                if n > 4:
                    with at.loop(act, n // 2 - 1, chunks=2, tiles=4):
                        two("plain")
                else:
                    two("plain")
                two(after)

            def operand(dst, src, z=True, scale=1.0):
                if z:
                    at.z += 1
                    act.wait_ge(z_done, at.z)
                act.activation(dst, src, ACT.Copy, scale=scale).then_inc(op_hi, 1)
                at.operand.next()

            def normed_h(l, mod, n_streams):
                for k in range(DT):
                    at.z += 1
                    act.wait_ge(z_done, at.z)
                    for s in range(n_streams):
                        last = act.activation(Hhi[:, k, half[s]], Z[:, k % 2, half[s]], ACT.Identity,
                                              bias=MOD[:, l, mod * DT + k, s:s + 1])
                    last.then_inc(op_hi, 1)
                    at.operand.next()

            t = at.tile()
            act.wait_ge(drained[t.bank], t.drained)
            act.activation(CTH[:, :], PAR[:, 3, CVEC:CVEC + 2 * DT], ACT.Tanh, scale=0.5).then_inc(cond_tanh, 1)
            look()
            for k in range(DT):
                t = copy_out(X[:, k, :])
                act.wait_ge(drained[t.bank], t.drained)
                square(X[:, k, :], T)
            root(T, D)
            mods(8)
            for l in range(DEPTH):
                TQ = NS[l] * SEQ
                normed_h(l, 0, 2)
                look("rope")
                for j in range(2):
                    t = at.tile()
                    act.wait_ge(tile_done, t.done)
                    square(banks[t.bank][:, :], T)
                look()
                at.tile()
                root(T, KVL)
                for k in range(2):
                    operand(Uhi[:, CT0 + k, :], Z[:, k % 2, :])
                look()
                for j in range(2):
                    t = at.tile()
                    act.wait_ge(tile_done, t.done)
                    square(banks[t.bank][:, 0:TQ], TQ)
                look()
                t = at.tile()
                act.wait_ge(tile_done, t.done)
                square(banks[t.bank][:, 0:TQ], TQ)
                look()
                for j in range(2):
                    copy_out(TG[:, j, 0:TQ], TQ, ACT.Tanh, 0.5)
                root(TQ, QL)
                for k in range(3):
                    operand(Uhi[:, QT + k, 0:TQ], Z[:, k % 2, 0:TQ])
                look()
                glu = [at.tile(), at.tile()]
                look()
                for j in range(2):
                    act.wait_ge(drained[glu[j].bank], glu[j].drained)
                    copy_out(TG[:, j, 0:TQ], TQ)
                look()
                at.tile()
                at.tile()
                look("plain" if l == 0 else "pair")
                for j in range(2):
                    copy_out(BG[:, j, 0:TQ], TQ)
                if l == 0:
                    mods(8, "pair")

                units = units_of(l)

                def pair(p, after):
                    look()
                    t = at.tile()
                    act.wait_ge(tile_done, t.done)
                    for h in range(2):
                        last = act.activation(Kb[0:NOPE, h, :], banks[t.bank][h * NOPE:(h + 1) * NOPE, :], ACT.Copy)
                    last.then_inc(drained[t.bank], 1)
                    for h in range(2):
                        t = at.tile()
                        act.wait_ge(tile_done, t.done)
                        act.activation(Qb[0:NOPE, h, 0:TQ], banks[t.bank][0:NOPE, 0:TQ], ACT.Copy,
                                       scale=SCALE).then_inc(q_nope, 1)
                    copy_out(V[:, :, :].rearrange("p t n -> p (t n)"))

                    def exps(u):
                        _, _, _, kt = units[u]
                        act.wait_ge(max_done, at.unit.now() + 1)
                        if u >= 2:
                            act.wait_ge(turned, at.unit.now() - 1)
                        act.activation(PR[:, u % 2, 0:kt * P], S[u % 2][:, 0:kt * P], ACT.Exp,
                                       bias=NM[:, u % 2:u % 2 + 1],
                                       accum_out=RS[:, u % 2:u % 2 + 1]).then_inc(exp_done, 1)
                        at.unit.next()

                    def copy_turned(u):
                        kt = units[u][3]
                        done = at.unit.now() - (n_done[0] - u) + 1
                        act.wait_ge(turned, done)
                        if u >= 2:
                            act.wait_ge(pv_done, done - 2)
                        act.activation(PTs[:, u % 2, 0:kt * P], PT[:, 0:kt * P], ACT.Copy).then_inc(turned_copied, 1)

                    n_done = [0]

                    def exps_(u):
                        exps(u)
                        n_done[0] += 1

                    exps_(0)
                    exps_(1)
                    copy_out(G[:, p * 2, 0:TQ], TQ, ACT.Tanh, 0.5)
                    look(after)
                    for u in range(2, len(units)):
                        copy_turned(u - 2)
                        exps_(u)
                    copy_turned(len(units) - 2)
                    copy_turned(len(units) - 1)
                    copy_out(G[:, p * 2 + 1, 0:TQ], TQ, ACT.Tanh, 0.5)
                    act.wait_ge(pv_done, at.unit.now())
                    act.activation(Uhi[:, p + AT0, 0:TQ], PV[:, 0:TQ], ACT.Copy).then_inc(op_hi, 1)
                    at.operand.next()

                with at.loop(act, PAIRS - 1, chunks=2, tiles=6, units=len(units), operands=1) as i:
                    pair(i, "pair")
                pair(PAIRS - 1, "plain")

                look()
                act.wait_ge(conv_a, l + 1)
                for j in range(2):
                    operand(Uhi[:, SO0 + j, 0:TQ], BG[:, j, 0:TQ], z=False)
                at.tile()
                at.tile()
                mean = at.tile()
                act.wait_ge(drained[mean.bank], mean.drained)
                for j in range(2):
                    last = act.activation(SQ[:, j, 0:TQ], ACC[:, j, 0:TQ], ACT.Square)
                last.then_inc(conv_sq, 1)
                at.tile()
                at.tile()
                root(TQ, CH)
                look()
                act.wait_ge(conv_v, l + 1)
                for j in range(2):
                    last = act.activation(TG[:, j, 0:TQ], ACC[:, j, 0:TQ], ACT.Tanh, scale=0.5)
                last.then_inc(conv_t, 1)
                act.wait_ge(conv_s, l + 1)
                for j in range(2):
                    operand(Uhi[:, CO0 + j, 0:TQ], Z[:, j, 0:TQ], z=False, scale=0.5)
                for _ in range(4):
                    at.tile()

                with at.loop(act, 4, chunks=4, tiles=8):
                    free = [(2 + j, at.uses[2 + j].now()) for j in range(2)]
                    for kind in ("quarter", "plain"):
                        for part in range(2):
                            if part == 0:
                                look("quarter")
                                for j in range(2):
                                    act.wait_ge(drained[free[j][0]], free[j][1])
                                    copy_out(TG[:, j, 0:TQ], TQ, ACT.Tanh, 0.5)
                            else:
                                look()
                                outs = [at.tile(), at.tile()]
                                free = [(t.bank, t.drained) for t in outs]
                summed = [u.now() for u in at.uses]
                if l == 0:
                    mods(4)
                for b in range(4):
                    act.wait_ge(drained[b], summed[b])
                for k in range(DT):
                    operand(Hhi[:, k, 0:TQ], G[:, k, 0:TQ], z=False, scale=0.5)

                def residual_squares(m):
                    t = at.tile()
                    act.wait_ge(drained[t.bank], t.drained)
                    square(X[:, m, 0:TQ], TQ)

                with at.loop(act, 2, chunks=2, tiles=4, squares=4) as i:
                    for j in range(2):
                        look()
                        for q in range(2):
                            residual_squares(i * 4 + (2 * j + q))
                root(TQ, D)
                if l == 0:
                    mods(4)
                normed_h(l, 3, NS[l])
                h0 = 0
                for g, n in enumerate(FF_GROUPS):
                    last = g == len(FF_GROUPS) - 1
                    with at.loop(act, n // 2, chunks=2, tiles=4, operands=2) as i:
                        look()
                        for j in range(2):
                            t = at.tile()
                            act.wait_ge(tile_done, t.done)
                            act.activation(TG[:, j, 0:TQ], banks[t.bank][:, 0:TQ], ACT.Tanh,
                                           scale=0.5).then_inc(gate_tanh, 1)
                        look()
                        for j in range(2):
                            t = at.tile()
                            act.wait_ge(drained[t.bank], t.drained)
                            act.activation(Uhi[:, i * 2 + j, 0:TQ], PR[:, j, 0:TQ],
                                           ACT.Copy).then_inc(op_hi, 1)
                            at.operand.next()
                    if l == 0:
                        mods(8)
                    end = last and l == DEPTH - 1
                    if end:
                        for j in range(4):
                            if j < 3:
                                look()
                            for q in range(2):
                                residual_squares(2 * j + q)
                    else:
                        with at.loop(act, 2, chunks=2, tiles=4, squares=4 * last) as i:
                            for j in range(2):
                                look()
                                for q in range(2):
                                    if last:
                                        residual_squares(i * 4 + (2 * j + q))
                                    else:
                                        at.tile()
                root(SEQ if l == DEPTH - 1 else T, D)
            act.wait_ge(fin_z, DT)
            for k in range(4):
                t = at.tile()
                act.wait_ge(tile_done, t.done)
                act.activation(X[:, k, :], banks[t.bank][:, :], ACT.Copy).then_inc(out_ready, 1)

        @block.vector
        def _(dve):
            at = Place()
            step = Tally()
            add, mult, sub = ALU.add, ALU.mult, ALU.subtract

            def mark(ins):
                ins.then_inc(dve_step, 1)
                return step.next()

            def after_all():
                dve.wait_ge(dve_step, step.now())

            def settle():
                after_all()
                if at.operand.n:
                    dve.wait_ge(op_lo, at.operand.now())

            def look(kind="plain"):
                split_lo(dve, 1, at, kind)

            def full():
                t = at.tile()
                dve.wait_ge(tile_done, t.done)
                return t

            def through(t):
                dve.wait_ge(drained[t.bank], t.drained)

            def mods(l, first, n, after="plain"):
                def two(chunk, after):
                    look()
                    look(after)
                    at.tile()
                    at.tile()
                    for j in range(2):
                        t = full()
                        for s in range(2):
                            last = dve.tensor_tensor(
                                MOD[:, l, bass.ds(chunk * 2 + 2 * j, 2), s],
                                banks[t.bank][:, 0:4].rearrange("p (f s) -> p f s", s=2)[:, :, s],
                                PAR[:, 2, bass.ds(chunk * 2 + (l * NMOD * DT + 2 * j), 2)], add)
                        last.then_inc(drained[t.bank], 1)
                    return t
                if n > 4:
                    with at.loop(dve, n // 2 - 1, chunks=2, tiles=4) as i:
                        two(i * 2 + first, "plain")
                else:
                    two(first, "plain")
                through(two(first + n - 2, after))

            def take_root(n, roots):
                t = at.tile()
                settle()
                dve.wait_ge(root_done, roots)
                dve.reciprocal(RSTD[:, 0:n], ROOT[:, 0:n]).then_inc(drained[t.bank], 1)
                through(t)

            def low(dst, src, hi, scale=None, shift=None):
                dve.wait_ge(op_hi, at.operand.now() + 1)
                if scale is not None:
                    ins = [dve.scalar_tensor_tensor(dst, src, scale, hi.bitcast(F32), mult, sub)]
                elif shift is not None:
                    ins = [dve.scalar_tensor_tensor(dst[:, h], src[:, h], b, hi[:, h].bitcast(F32), add, sub)
                           for h, b in shift]
                else:
                    ins = [dve.tensor_tensor(dst, src, hi.bitcast(F32), sub)]
                ins[-1].then_inc(op_lo, 1)
                at.operand.next()

            def normed_h(l, mod, gain, n_streams):
                settle()
                for s in range(n_streams):
                    mark(dve.scalar_tensor_tensor(AV[:, :, s], MOD[:, l, (mod + 1) * DT:(mod + 2) * DT, s], 1.0,
                                                  PAR[:, l, gain:gain + DT], add, mult))
                after_all()

                def low_part(k):
                    low(Hlo[:, k, :], Z[:, k % 2, :], Hhi[:, k, :],
                        shift=[(half[s], MOD[:, l, mod * DT + k, s:s + 1]) for s in range(n_streams)])

                for k in range(DT):
                    settle()
                    for s in range(n_streams):
                        last = dve.scalar_tensor_tensor(Z[:, k % 2, half[s]], X[:, k, half[s]], AV[:, k, s:s + 1],
                                                        RSTD[:, half[s]], mult, mult)
                    last.then_inc(z_done, 1)
                    if k:
                        low_part(k - 1)
                low_part(DT - 1)

            def normed(l, n, tiles, raw0, to, gain):
                def low_part(k):
                    low(Ulo[:, to + k, 0:n], Z[:, k % 2, 0:n], Uhi[:, to + k, 0:n])

                for k in range(tiles):
                    settle()
                    dve.scalar_tensor_tensor(Z[:, k % 2, 0:n], G[:, raw0 + k, 0:n],
                                             PAR[:, l, gain + k:gain + k + 1], RSTD[:, 0:n],
                                             mult, mult).then_inc(z_done, 1)
                    if k:
                        low_part(k - 1)
                low_part(tiles - 1)

            def keep_raw(k, n):
                t = full()
                dve.wait_ge(sq_done, at.square.next())
                dve.tensor_copy(G[:, k, 0:n], banks[t.bank][:, 0:n]).then_inc(drained[t.bank], 1)

            t = full()
            for b, n in enumerate((ROWS, ROWS, 2 * NMOD * DT, CVEC + 2 * DT)):
                last = dve.tensor_copy(PAR[:, b, 0:n], banks[t.bank][:, b * P:b * P + n])
            last.then_inc(drained[t.bank], 1)
            dve.wait_ge(cond_tanh, 1)
            CSf = CS[:, :, :].rearrange("p s k -> p (s k)")
            mark(dve.scalar_tensor_tensor(CSf, CTH[:, :], 1.0, PAR[:, 3, CVEC:CVEC + 2 * DT], add, mult))
            after_all()
            cv = [CV[:, :, 2 * j:2 * j + 2].rearrange("p k s -> p s k") for j in range(2)]
            mark(dve.tensor_scalar(cv[0], CS[:, :, :], 0.5, None, mult))
            after_all()
            dve.scalar_tensor_tensor(cv[1], CS[:, :, :], 0.5, cv[0].bitcast(F32), mult, sub).then_inc(cond_done, 1)
            look()
            for _ in range(DT):
                at.tile()
                at.square.next()
            take_root(T, stat_root(0, 0))
            mods(0, 0, 8)
            dve.wait_ge(consts, 4)
            for l in range(DEPTH):
                TQ = NS[l] * SEQ
                normed_h(l, 0, LN1, 2)
                look("rope")
                keep_raw(0, T)
                keep_raw(1, T)
                look()
                settle()
                t = full()
                mark(dve.tensor_tensor(Z[64:96, 0, :], banks[t.bank][0:32, :], TAB[0:32, :], mult))
                dve.tensor_tensor(Z[64:96, 1, :], banks[t.bank][32:64, :], TAB[32:64, :], mult).then_inc(
                    drained[t.bank], 1)
                after_all()
                through(t)
                for h in range(2):
                    mark(dve.tensor_tensor(Kb[64:96, h, :], Z[64:96, 0, :], Z[64:96, 1, :], add))
                take_root(T, stat_root(l, 1))
                normed(l, T, 2, 0, CT0, KVG)
                look()
                keep_raw(2, TQ)
                keep_raw(3, TQ)
                look()
                keep_raw(4, TQ)
                look()
                tanh_g = [at.tile(), at.tile()]
                take_root(TQ, stat_root(l, 2))
                normed(l, TQ, 3, 2, QT, QG)
                look()
                for j in range(2):
                    t = full()
                    dve.wait_ge(drained[tanh_g[j].bank], tanh_g[j].drained)
                    dve.scalar_tensor_tensor(U[:, j, 0:NS[l], PAD:PAD + SEQ], by_stream(TG[:, j, :], l), 1.0,
                                             by_stream(banks[t.bank][:, :], l), add, mult).then_inc(
                                                 drained[t.bank], 1)
                look()
                through(t)

                def tap(w, start):
                    for j in range(2):
                        dve.wait_ge(dve_step, step.now() - 1)
                        mark(dve.scalar_tensor_tensor(
                            by_stream(ACC[:, j, :], l), U[:, j, 0:NS[l], bass.ds(start, SEQ)],
                            PAR[:, l, bass.ds(w + j, 1)], by_stream(ACC[:, j, :], l), mult, add))

                for j in range(2):
                    mark(dve.tensor_scalar(by_stream(ACC[:, j, :], l), U[:, j, 0:NS[l], 0:SEQ],
                                           PAR[:, l, CDW + j:CDW + j + 1], None, mult))
                gates = [at.tile(), at.tile()]
                look()
                for j in range(2):
                    t = full()
                    dve.wait_ge(drained[gates[j].bank], gates[j].drained)
                    dve.tensor_tensor(C[:, j, 0:NS[l], 1:1 + SEQ], by_stream(TG[:, j, :], l),
                                      by_stream(banks[t.bank][:, :], l), mult).then_inc(drained[t.bank], 1)
                look("plain" if l == 0 else "pair")
                through(t)
                for w in range(SC_TAPS):
                    for j in range(2):
                        wt = PAR[:, l, SCW + 2 * w + j:SCW + 2 * w + j + 1]
                        src, acc = C[:, j, 0:NS[l], w:w + SEQ], by_stream(Z[:, j, :], l)
                        if w == 0:
                            mark(dve.tensor_scalar(acc, src, wt, None, mult))
                        else:
                            dve.wait_ge(dve_step, step.now() - 1)
                            mark(dve.scalar_tensor_tensor(acc, src, wt, acc, mult, add))
                for j in range(2):
                    t = at.tile()
                    dve.wait_ge(drained[t.bank], t.drained)
                    dve.wait_ge(dve_step, step.now() - 1 + j)
                    mark(dve.tensor_tensor(BG[:, j, 0:TQ], BG[:, j, 0:TQ], Z[:, j, 0:TQ], mult))
                for w in range(1, TAPS_BEFORE):
                    tap(CDW + 2 * w, w)
                if l == 0:
                    mods(0, 8, 8, "pair")

                units = units_of(l)

                def pair(p, after):
                    look()
                    at.tile()
                    after_all()
                    for h in range(2):
                        t = full()
                        bank = banks[t.bank]
                        if h:
                            dve.wait_ge(q_ready, at.heads.now())
                        mark(dve.scalar_tensor_tensor(Z[64:96, 0, 0:TQ], bank[64:96, 0:TQ], SCALE,
                                                      TAB[64:96, 0:TQ], mult, mult))
                        dve.wait_ge(q_nope, at.heads.next())
                        dve.scalar_tensor_tensor(Z[64:96, 1, 0:TQ], bank[96:128, 0:TQ], SCALE,
                                                 TAB[96:128, 0:TQ], mult, mult).then_inc(drained[t.bank], 1)
                        after_all()
                        through(t)
                        dve.tensor_tensor(Qb[64:96, h, 0:TQ], Z[64:96, 0, 0:TQ], Z[64:96, 1, 0:TQ],
                                          add).then_inc(q_ready, 1)
                    at.tile()
                    taps = iter(range(TAPS_BEFORE, TAPS_BEFORE + TAPS_PER_PAIR))

                    def do_taps(n):
                        for w in [next(taps) for _ in range(n)]:
                            tap(p * (2 * TAPS_PER_PAIR) + (CDW + 2 * w), p * TAPS_PER_PAIR + w)

                    do_taps(1)
                    base = at.unit.n

                    def unit(k):
                        return at.unit.now() - (at.unit.n - base) + k

                    def row_max(u):
                        kt = units[u][3]
                        dve.wait_ge(qk_done, unit(u + 1))
                        dve.tensor_reduce(NM[:, u % 2:u % 2 + 1], S[u % 2][:, 0:kt * P], AX.X, ALU.max,
                                          negate=True).then_inc(max_done, 1)

                    def normalise(u):
                        kt = units[u][3]
                        dve.wait_ge(exp_done, unit(u + 1))
                        mark(dve.reciprocal(RR[:, u % 2:u % 2 + 1], RS[:, u % 2:u % 2 + 1]))
                        after_all()
                        dve.tensor_scalar(PR[:, u % 2, 0:kt * P], PR[:, u % 2, 0:kt * P],
                                          RR[:, u % 2:u % 2 + 1], None, mult).then_inc(prob_done, 1)

                    row_max(0)
                    row_max(1)
                    normalise(0)
                    look(after)
                    per = (TAPS_PER_PAIR - 1) // (len(units) - 2)
                    for u in range(2, len(units)):
                        row_max(u)
                        normalise(u - 1)
                        do_taps(per)
                    normalise(len(units) - 1)
                    for _ in units:
                        at.unit.next()
                    at.tile()
                    at.tile()
                    low(Ulo[:, p + AT0, 0:TQ], PV[:, 0:TQ], Uhi[:, p + AT0, 0:TQ])

                steps = 2 + 2 * TAPS_PER_PAIR + len(units)
                with at.loop(dve, PAIRS - 1, chunks=2, tiles=6, units=len(units), operands=1, heads=2,
                             extra=[(step, steps)]) as i:
                    pair(i, "pair")
                pair(PAIRS - 1, "plain")

                def attended(m):
                    t = full()
                    dve.scalar_tensor_tensor(G[:, m, 0:TQ], G[:, m, 0:TQ], 1.0, banks[t.bank][:, 0:TQ],
                                             add, mult).then_inc(drained[t.bank], 1)

                look()
                after_all()
                for j in range(2):
                    last = dve.tensor_scalar(ACC[:, j, 0:TQ], ACC[:, j, 0:TQ], 0.5,
                                             PAR[:, l, CB + j:CB + j + 1], mult, add)
                last.then_inc(conv_a, 1)
                for j in range(2):
                    low(Ulo[:, SO0 + j, 0:TQ], BG[:, j, 0:TQ], Uhi[:, SO0 + j, 0:TQ])
                attended(0)
                attended(1)
                t = full()
                dve.wait_ge(conv_a, l + 1)
                for j in range(2):
                    last = dve.scalar_tensor_tensor(ACC[:, j, 0:TQ], banks[t.bank][:, 0:TQ], -1.0 / CH,
                                                    ACC[:, j, 0:TQ], mult, add)
                last.then_inc(drained[t.bank], 1)
                attended(2)
                attended(3)
                take_root(TQ, stat_root(l, 3))
                look()
                for j in range(2):
                    mark(dve.tensor_tensor(Z[:, j, 0:TQ], ACC[:, j, 0:TQ], RSTD[:, 0:TQ], mult))
                after_all()
                for j in range(2):
                    last = dve.tensor_scalar(ACC[:, j, 0:TQ], Z[:, j, 0:TQ], PAR[:, l, LNG + j:LNG + j + 1],
                                             PAR[:, l, LNB + j:LNB + j + 1], mult, add)
                last.then_inc(conv_v, 1)
                dve.wait_ge(conv_t, l + 1)
                dve.wait_ge(conv_v, l + 1)
                for j in range(2):
                    last = dve.scalar_tensor_tensor(Z[:, j, 0:TQ], TG[:, j, 0:TQ], 1.0, ACC[:, j, 0:TQ], add, mult)
                last.then_inc(conv_s, 1)
                for j in range(2):
                    low(Ulo[:, CO0 + j, 0:TQ], Z[:, j, 0:TQ], Uhi[:, CO0 + j, 0:TQ], scale=0.5)
                for m in range(4, DT):
                    attended(m)

                settle()
                with at.loop(dve, 4, chunks=4, tiles=8, extra=[(step, 4)]) as i:
                    free = [(2 + j, at.uses[2 + j].now()) for j in range(2)]
                    for branch in range(2):
                        look("quarter")
                        gates = [at.tile(), at.tile()]
                        look()
                        for j in range(2):
                            t = full()
                            dve.wait_ge(drained[gates[j].bank], gates[j].drained)
                            dve.wait_ge(drained[free[j][0]], free[j][1])
                            mark(dve.scalar_tensor_tensor(Z[:, j, 0:TQ], TG[:, j, 0:TQ], 1.0,
                                                          banks[t.bank][:, 0:TQ], add, mult))
                            after_all()
                            m = i * 2 + j
                            dve.tensor_tensor(G[:, m, 0:TQ], G[:, m, 0:TQ], Z[:, j, 0:TQ], add).then_inc(
                                drained[t.bank], 1)
                            free[j] = (t.bank, t.drained)
                if l == 0:
                    mods(0, 16, 4)
                for k in range(DT):
                    low(Hlo[:, k, 0:TQ], G[:, k, 0:TQ], Hhi[:, k, 0:TQ], scale=0.5)

                def residual(m, mod):
                    t = full()
                    for s in range(NS[l]):
                        last = dve.scalar_tensor_tensor(X[:, m, half[s]], banks[t.bank][:, half[s]],
                                                        MOD[:, l, m + mod * DT, s:s + 1], X[:, m, half[s]],
                                                        mult, add)
                    last.then_inc(drained[t.bank], 1)
                    return t

                with at.loop(dve, 2, chunks=2, tiles=4) as i:
                    for j in range(2):
                        look()
                        for q in range(2):
                            residual(i * 4 + (2 * j + q), 2)
                at.square.n += DT
                take_root(TQ, stat_root(l, 4))
                if l == 0:
                    mods(0, 20, 4)
                normed_h(l, 3, LN2, NS[l])
                for g, n in enumerate(FF_GROUPS):
                    last_group = g == len(FF_GROUPS) - 1
                    with at.loop(dve, n // 2, chunks=2, tiles=4, operands=2, gates=2) as i:
                        free = [at.uses[2 + j].now() for j in range(2)]
                        look()
                        for j in range(2):
                            t = full()
                            dve.wait_ge(gate_tanh, at.gates.next())
                            dve.wait_ge(drained[2 + j], free[j])
                            dve.scalar_tensor_tensor(Z[:, j, 0:TQ], TG[:, j, 0:TQ], 1.0, banks[t.bank][:, 0:TQ],
                                                     add, mult).then_inc(drained[t.bank], 1)
                        look()
                        through(t)
                        dve.wait_ge(op_lo, at.operand.now())
                        for j in range(2):
                            t = full()
                            dve.scalar_tensor_tensor(PR[:, j, 0:TQ], Z[:, j, 0:TQ], 0.5, banks[t.bank][:, 0:TQ],
                                                     mult, mult).then_inc(drained[t.bank], 1)
                        for j in range(2):
                            low(Ulo[:, i * 2 + j, 0:TQ], PR[:, j, 0:TQ], Uhi[:, i * 2 + j, 0:TQ])
                    if l == 0:
                        mods(1, 8 * g, 8)
                    if last_group and l == DEPTH - 1:
                        for j in range(4):
                            if j < 3:
                                look()
                            for q in range(2):
                                residual(2 * j + q, 5)
                    else:
                        with at.loop(dve, 2, chunks=2, tiles=4) as i:
                            for j in range(2):
                                look()
                                for q in range(2):
                                    residual(i * 4 + (2 * j + q), 5)
                at.square.n += DT
                take_root(T if l == 0 else SEQ, stat_root(l + 1, 0))
            for k in range(DT):
                dve.scalar_tensor_tensor(G[:, k, 0:SEQ], X[:, k, 0:SEQ], PAR[:, 3, FING + k:FING + k + 1],
                                         RSTD[:, 0:SEQ], mult, mult).then_inc(fin_z, 1)

        @block.tensor
        def _(pe):
            at = Place()

            def new_tile():
                t = at.tile()
                if not isinstance(t.before, int) or t.before > 0:
                    pe.wait_ge(drained[t.bank], t.before)
                return t

            def chunk():
                slot, n = at.chunk.n % 2, at.chunk.n
                if at.chunk.var is None:
                    pe.wait_ge(lo_done[slot], n // 2 + 1)
                else:
                    pe.wait_ge(lo_done[slot], at.chunk.var * (at.chunk.step // 2) + (n // 2 + 1))
                at.chunk.next()
                return slot

            def split_product(dst, k, terms, ready=None):
                for j in range(k):
                    if ready is not None:
                        pe.wait_ge(op_lo, ready + j + 1)
                    sh, sl, mh, ml = terms(j)
                    pe.matmul(dst, sh, mh, start=j == 0, stop=False)
                    pe.matmul(dst, sh, ml, start=False, stop=False)
                    last = pe.matmul(dst, sl, mh, start=False, stop=j == k - 1)
                return last

            def gemm(slot, width, col, m, k, ops, o0, n, ready=None):
                t = new_tile()
                oh, ol = ops

                def terms(j):
                    a = j * width + col
                    return (Whi[:, slot, a:a + m], Wlo[:, slot, a:a + m],
                            oh[:, o0 + j, 0:n], ol[:, o0 + j, 0:n])

                last = split_product(banks[t.bank][0:m, 0:n], k, terms, ready)
                return t, last

            H, O = (Hhi, Hlo), (Uhi, Ulo)

            def tiles_of(width, n_tiles, m, k, ops, o0, n, ready=None):
                slot = chunk()
                for q in range(n_tiles):
                    _, last = gemm(slot, width, q * m, m, k, ops, o0, n, ready)
                    last.then_inc(tile_done, 1)

            def total(n):
                pe.wait_ge(sq_summed, at.square.now())
                t = new_tile()
                pe.matmul(banks[t.bank][:, 0:n], ONES[:, :], SUM[:, 0:n], start=True, stop=True).then_inc(tile_done, 1)

            def mods(n):
                def two():
                    rows = []
                    for j in range(2):
                        slot = chunk()
                        t = new_tile()
                        for k in range(DT):
                            for w in (Whi, Wlo):
                                last = pe.matmul(banks[t.bank][0:4, 0:CW], CV[:, k, :],
                                                 w[:, slot, k * CW:(k + 1) * CW],
                                                 start=k == 0 and w is Whi, stop=k == DT - 1 and w is Wlo)
                        last.then_inc(tile_done, 1)
                        rows.append(t)
                    for j in range(2):
                        t = new_tile()
                        pe.wait_ge(drained[rows[j].bank], rows[j].drained)
                        for f in range(2):
                            last = pe.matmul(banks[t.bank][:, 2 * f:2 * f + 2], ROW[:, j, f * P:(f + 1) * P],
                                             SEL[:, :], start=True, stop=True)
                        last.then_inc(tile_done, 1)
                if n > 4:
                    with at.loop(pe, n // 2 - 1, chunks=2, tiles=4):
                        two()
                else:
                    two()
                two()

            pe.wait_ge(consts, 4)
            pe.wait_ge(vec_in, 16 * N_VEC)
            t = new_tile()
            for b, n in enumerate((ROWS, ROWS, 2 * NMOD * DT, CVEC + 2 * DT)):
                last = pe.transpose(banks[t.bank][:, b * P:b * P + n], PST[0:n, 0, b * P:(b + 1) * P], IDN[0:n, 0:n])
            last.then_inc(tile_done, 1)
            pe.wait_ge(x_in, 32)
            for k in range(DT):
                t = new_tile()
                for j in range(4):
                    src = G[:, 2 * j + k // 4, (k % 4) * P:(k % 4 + 1) * P]
                    last = pe.transpose(banks[t.bank][:, j * P:(j + 1) * P], src, IDN[:, :])
                last.then_inc(tile_done, 1)
                at.square.next()
            total(T)
            pe.wait_ge(cond_done, 1)
            mods(8)
            for l in range(DEPTH):
                TQ = NS[l] * SEQ
                o = at.operand.n
                tiles_of(CW, 2, P, DT, H, 0, T, o)
                at.square.n += 2
                tiles_of(2 * ROPE, 1, 2 * ROPE, DT, H, 0, T)
                total(T)
                tiles_of(CW, 2, P, DT, H, 0, TQ)
                tiles_of(QL - CW, 1, P, DT, H, 0, TQ)
                at.square.n += 3
                tiles_of(CW, 2, P, DT, H, 0, TQ)
                total(TQ)
                for _ in range(4):
                    tiles_of(CW, 2, P, DT, H, 0, TQ)
                at.operand.n += DT + 5
                if l == 0:
                    mods(8)

                units = units_of(l)

                def gate_tile(slot, q):
                    _, last = gemm(slot, CW, q * P, P, DT, H, 0, TQ)
                    last.then_inc(tile_done, 1)

                def pair(first):
                    slot = chunk()
                    wq = [pair_views(w, slot, True)[0] for w in (Whi, Wlo)]
                    wkv = [pair_views(w, slot, True)[1].rearrange("p (k e n) -> p k e n", k=2, e=2)
                           for w in (Whi, Wlo)]
                    pe.wait_ge(op_lo, at.operand.now())
                    keys = new_tile()
                    split_product(banks[keys.bank][:, :], 2,
                                  lambda k: (wkv[0][:, k, 0, :], wkv[1][:, k, 0, :],
                                             Uhi[:, CT0 + k, :], Ulo[:, CT0 + k, :])).then_inc(tile_done, 1)
                    for h in range(2):
                        t = new_tile()
                        split_product(banks[t.bank][:, 0:TQ], 3,
                                      lambda k: (wq[0][:, 2 * k + h, :], wq[1][:, 2 * k + h, :],
                                                 Uhi[:, QT + k, 0:TQ], Ulo[:, QT + k, 0:TQ])).then_inc(tile_done, 1)
                    values = new_tile()
                    for tt in range(4):
                        cols = slice(tt * P, (tt + 1) * P)
                        last = split_product(banks[values.bank][:, cols], 2,
                                             lambda k: (Uhi[:, CT0 + k, cols], Ulo[:, CT0 + k, cols],
                                                        wkv[0][:, k, 1, :], wkv[1][:, k, 1, :]))
                    last.then_inc(tile_done, 1)
                    slot = chunk()
                    base = at.unit.n

                    def unit(k):
                        return at.unit.now() - (at.unit.n - base) + k

                    pe.wait_ge(drained[keys.bank], keys.drained)
                    pe.wait_ge(drained[values.bank], values.drained)
                    q0 = at.heads.now()

                    def scores(u):
                        h, col, k0, kt = units[u]
                        pe.wait_ge(q_ready, q0 + h + 1)
                        if u >= 2:
                            pe.wait_ge(exp_done, unit(u - 1))
                        pe.matmul(S[u % 2][:, 0:kt * P], Qb[:, h, col:col + P], Kb[:, h, k0 * P:(k0 + kt) * P],
                                  start=True, stop=True).then_inc(qk_done, 1)

                    def turn(u):
                        kt = units[u][3]
                        pe.wait_ge(prob_done, unit(u + 1))
                        if u:
                            pe.wait_ge(turned_copied, unit(u))
                        for k in range(kt):
                            last = pe.transpose(PT[:, k * P:(k + 1) * P], PR[:, u % 2, k * P:(k + 1) * P], IDN[:, :])
                        last.then_inc(turned, 1)

                    def values_of(u):
                        h, col, k0, kt = units[u]
                        pe.wait_ge(turned_copied, unit(u + 1))
                        for k in range(kt):
                            last = pe.matmul(PV[h * VH:(h + 1) * VH, col:col + P], V[:, k0 + k, h * VH:(h + 1) * VH],
                                             PTs[:, u % 2, k * P:(k + 1) * P], start=k == 0, stop=k == kt - 1)
                        last.then_inc(pv_done, 1)

                    n = len(units)
                    scores(0)
                    scores(1)
                    gate_tile(slot, 0)
                    for u in range(2, n):
                        scores(u)
                        turn(u - 2)
                        if u > 2:
                            values_of(u - 3)
                    turn(n - 2)
                    values_of(n - 3)
                    gate_tile(slot, 1)
                    turn(n - 1)
                    values_of(n - 2)
                    values_of(n - 1)
                    for _ in units:
                        at.unit.next()
                    at.heads.next()
                    at.heads.next()
                    at.operand.next()

                with at.loop(pe, PAIRS - 1, chunks=2, tiles=6, units=len(units), operands=1, heads=2) as i:
                    pair(i)
                pair(None)

                pe.wait_ge(op_lo, at.operand.n)
                slot = chunk()

                def mla(slot, q):
                    _, last = gemm(slot, 512, q * P, P, 4, O, AT0, TQ)
                    last.then_inc(tile_done, 1)

                def over_channels(src):
                    t = new_tile()
                    for j in range(2):
                        last = pe.matmul(banks[t.bank][:, 0:TQ], ONES[:, :], src[:, j, 0:TQ], start=j == 0, stop=j == 1)
                    last.then_inc(tile_done, 1)

                mla(slot, 0)
                mla(slot, 1)
                pe.wait_ge(conv_a, l + 1)
                over_channels(ACC)
                mla(slot, 2)
                mla(slot, 3)
                pe.wait_ge(conv_sq, l + 1)
                over_channels(SQ)
                slot = chunk()
                for q in range(4):
                    mla(slot, q)
                at.operand.n += 4

                with at.loop(pe, 4, chunks=4, tiles=8):
                    for o0 in (CO0, SO0):
                        tiles_of(CW, 2, P, DT, H, 0, TQ)
                        pe.wait_ge(op_lo, at.operand.n)
                        tiles_of(CW, 2, P, 2, O, o0, TQ)
                if l == 0:
                    mods(4)
                o = at.operand.n
                at.operand.n += DT
                with at.loop(pe, 2, chunks=2, tiles=4):
                    for j in range(2):
                        tiles_of(CW, 2, P, DT, H, 0, TQ, o)
                at.square.n += DT
                total(TQ)
                if l == 0:
                    mods(4)
                o = at.operand.n
                at.operand.n += DT
                for g, n in enumerate(FF_GROUPS):
                    with at.loop(pe, n // 2, chunks=2, tiles=4, operands=2):
                        for j in range(2):
                            tiles_of(CW, 2, P, DT, H, 0, TQ, o)
                            at.operand.next()
                    if l == 0:
                        mods(8)
                    up = at.operand.n - n
                    if g == len(FF_GROUPS) - 1 and l == DEPTH - 1:
                        for j in range(4):
                            tiles_of(CW, 2, P, n, O, 0, TQ, up)
                    else:
                        with at.loop(pe, 2, chunks=2, tiles=4):
                            for j in range(2):
                                tiles_of(CW, 2, P, n, O, 0, TQ, up)
                at.square.n += DT
                total(SEQ if l == DEPTH - 1 else T)
            pe.wait_ge(fin_z, DT)
            for j in range(2):
                for h in range(2):
                    t = new_tile()
                    for k in range(4):
                        last = pe.transpose(banks[t.bank][:, k * P:(k + 1) * P],
                                            G[:, 4 * h + k, j * P:(j + 1) * P], IDN[:, :])
                    last.then_inc(tile_done, 1)


_INS = ["x", "c", "ctx", "c_ctx", "w_mod", "b_mod", "ln1_g", "w_in", "q_a_norm_g", "w_q_b", "kv_a_norm_g",
        "w_kv_b", "w_mla_o", "conv_dw", "conv_dw_b", "conv_ln_g", "conv_ln_b", "w_conv_o", "sc_dw", "w_sc_o",
        "w_o", "ln2_g", "w_ff1", "w_ff3", "w_ff2", "final_g"]


def kernel(**inputs):
    import numpy as np
    import concourse.bacc as bacc
    from concourse.bass_utils import run_bass_kernel_spmd

    nc = bacc.Bacc("TRN2", target_bir_lowering=False, num_devices=1)
    arrays, args = {}, []
    for name in _INS:
        a = np.ascontiguousarray(inputs[name])
        arrays[f"in_{name}"] = a
        args.append(nc.dram_tensor(f"in_{name}", a.shape, mybir.dt.from_np(a.dtype), kind="ExternalInput").ap())
    token = np.arange(SEQ)
    inv = np.power(np.float32(10000.0), -np.arange(0, ROPE // 2, 2, dtype=np.float32) / np.float32(ROPE // 2))
    cos, sin = np.ones((ROPE, T), np.float32), np.zeros((ROPE, T), np.float32)
    for r in range(ROPE):
        pos = (token // GRID_W if r < ROPE // 2 else token % GRID_W).astype(np.float32)
        angle = pos * inv[r % 8]
        cos[r, :SEQ] = np.cos(angle)
        sin[r, :SEQ] = np.sin(angle) * (-1 if r % 16 < 8 else 1)
    arrays["rope"] = np.concatenate([cos, sin, cos, sin])
    args.append(nc.dram_tensor("rope", (P, T), mybir.dt.float32, kind="ExternalInput").ap())
    args.append(nc.dram_tensor("out", (1, SEQ, D), mybir.dt.float32, kind="ExternalOutput").ap())
    build(nc, *args)
    r = run_bass_kernel_spmd(nc, [arrays], core_ids=[0])
    return r.results[0]["out"]
```

```python
import math
from contextlib import ExitStack, contextmanager

import concourse.bass as bass
from concourse import mybir

D = 1024
SEQ = 256
DEPTH = 2
HEADS, NOPE, ROPE, VH = 8, 64, 32, 64
QL, KVL = 384, 256
CH = 256
TAPS, SC_TAPS = 31, 3
FF = 2816
GRID_W = 64
EPS = 1e-6
P = 128
DT = D // P
T = 2 * SEQ
KV0 = QL
ROPE0 = KV0 + KVL
GLU0 = ROPE0 + ROPE
SC0 = GLU0 + 2 * CH
GATE0 = SC0 + 3 * CH
SCALE = (NOPE + ROPE) ** -0.5
CW = P
SLOTS = 4
SLOT = DT * CW
NMOD = 6
GROUP = 4

LN1, LN2, QG, KVG, CB, LNG, LNB, CDW, SCW = 0, 8, 16, 19, 21, 23, 25, 27, 27 + 2 * TAPS
ROWS = SCW + 2 * SC_TAPS
N_VEC = 9 + 1 + 1
FING, CVEC = 0, 8
TAPS_BEFORE, TAPS_PER_PAIR = 3, 7
PAIRS = HEADS // 2
FF_GROUPS = [8, 8, 6]


PAIR_KINDS = ["keys", "queries", "plain", "plain"]


def with_mods(kinds, l):
    return [x for k in kinds for x in ((["plain", k]) if l == 0 and k in ("plain", "rope") else [k])]


def projection_kinds(l):
    return with_mods(["plain", "plain", "rope"] + ["plain"] * 13, l)


def branch_kinds(l):
    return with_mods(["plain", "plain", "short", "short"] * 2, l)


def ahead(kinds, after):
    return iter((kinds + after)[2:])


class Tally:

    def __init__(self):
        self.n, self.var, self.step = 0, None, 0

    def now(self):
        return self.n if self.var is None else self.var * self.step + self.n

    def next(self):
        self.n += 1
        return self.now()


@contextmanager
def turns(eng, times, steps):
    before = [(t, t.n, k) for t, k in steps]
    with eng.Fori(0, times) as i:
        for t, _, k in before:
            t.var, t.step = i, k
        yield i
    for t, n, k in before:
        assert t.n - n == k, (t.n - n, k, steps.index((t, k)))
        t.n, t.var, t.step = n + k * times, None, 0


class Tile:

    def __init__(self, bank, done, before, drained):
        self.bank, self.done, self.before, self.drained = bank, done, before, drained


class Place:

    def __init__(self):
        self.chunk, self.tiles, self.operand, self.unit, self.square, self.heads, self.gates, self.group = (Tally() for _ in range(8))
        self.uses = [Tally() for _ in range(4)]
        self.ring = 0
        self.z = 0

    def tile(self):
        b = self.ring % 4
        self.ring += 1
        before = self.uses[b].now()
        return Tile(b, self.tiles.next(), before, self.uses[b].next())

    @contextmanager
    def loop(self, eng, times, chunks=0, tiles=0, operands=0, units=0, squares=0, heads=0, gates=0, groups=0, extra=()):
        self.ring = 0
        steps = [(self.chunk, chunks), (self.tiles, tiles), (self.operand, operands),
                 (self.unit, units), (self.square, squares), (self.heads, heads), (self.gates, gates), (self.group, groups), *extra]
        steps += [(u, (tiles - b + 3) // 4 if tiles > b else 0) for b, u in enumerate(self.uses)]
        assert times > 1 and chunks % SLOTS == 0
        with turns(eng, times, steps) as i:
            yield i
        self.ring = 0


def build(nc, x, c, ctx_in, c_ctx, w_mod, b_mod, ln1_g, w_in, q_a_norm_g, w_q_b, kv_a_norm_g,
          w_kv_b, w_mla_o, conv_dw, conv_dw_b, conv_ln_g, conv_ln_b, w_conv_o, sc_dw, w_sc_o,
          w_o, ln2_g, w_ff1, w_ff3, w_ff2, final_g, rope, out):
    F32, F32R = mybir.dt.float32, mybir.dt.float32r
    ACT, ALU, AX = mybir.ActivationFunctionType, mybir.AluOpType, mybir.AxisListType

    stack = ExitStack()
    with stack:
        def sb(name, shape, dt=F32):
            return stack.enter_context(nc.sbuf_tensor(name, shape, dt))

        def sem(name):
            return stack.enter_context(nc.semaphore(name))

        X = sb("X", [P, DT, T])
        Wraw = sb("Wraw", [P, SLOTS, SLOT])
        Whi = sb("Whi", [P, SLOTS, SLOT], F32R)
        Wlo = sb("Wlo", [P, SLOTS, SLOT], F32R)
        Hhi = sb("Hhi", [P, DT, T], F32R)
        Hlo = sb("Hlo", [P, DT, T], F32R)
        G = sb("G", [P, DT, T])
        Uhi = sb("Uhi", [P, 9, T], F32R)
        Ulo = sb("Ulo", [P, 9, T], F32R)
        QT, CT0, AT0, CO0, SO0 = 0, 3, 5, 0, 2
        Qb = sb("Qb", [96, 2, T])
        Kb = sb("Kb", [96, 2, T])
        V = sb("V", [P, 4, P])
        PR = sb("PR", [P, 2, T])
        PTs = sb("PTs", [P, 2, T])
        PAD = TAPS // 2
        U = sb("U", [P, 2, 2, SEQ + 2 * PAD])
        ACC = sb("ACC", [P, 2, T])
        C = sb("C", [P, 2, 2, SEQ + 2])
        BG = sb("BG", [P, 2, T])
        SQ = sb("SQ", [P, 2, T])
        SUM = sb("SUM", [P, T])
        ROOT = sb("ROOT", [P, T])
        RSTD = sb("RSTD", [P, T])
        Z = sb("Z", [P, 2, T])
        TG = sb("TG", [P, 2, T])
        TAB = sb("TAB", [P, T])
        IDN = sb("IDN", [P, P])
        ONES = sb("ONES", [P, P])
        PAR = sb("PAR", [P, 4, P])
        MOD = sb("MOD", [P, DEPTH, NMOD * DT, 2])
        AV = sb("AV", [P, DT, 2])
        CTH = sb("CTH", [P, 16])
        CS = sb("CS", [P, 2, DT])
        CV = sb("CV", [P, DT, 4], F32R)
        SEL = sb("SEL", [4, 2])
        ROW = PTs[0:4, 0, :]
        NM = sb("NM", [P, 2])
        RS = sb("RS", [P, 2])
        RR = sb("RR", [P, 2])
        PST = TG

        banks = [stack.enter_context(nc.psum_tensor(f"bank{b}", [P, T], F32)) for b in range(4)]
        S = [stack.enter_context(nc.psum_tensor(f"scores{b}", [P, T], F32)) for b in range(2)]
        PT = stack.enter_context(nc.psum_tensor("probsT", [P, T], F32))
        PV = stack.enter_context(nc.psum_tensor("attended", [P, T], F32))

        x_in = sem("x_in")
        shared_in = sem("shared_in")
        vec_in = sem("vec_in")
        consts = sem("consts")
        raw_in = [sem(f"raw_in{b}") for b in range(SLOTS)]
        slot_free = sem("slot_free")
        hi_done = sem("hi_done")
        lo_done = [sem(f"lo_done{b}") for b in range(SLOTS)]
        mod_used = sem("mod_used")
        mod_rows = sem("mod_rows")
        mod_cols = sem("mod_cols")
        mod_done = sem("mod_done")
        tile_done = sem("tile_done")
        drained = [sem(f"drained{b}") for b in range(4)]
        sq_done = sem("sq_done")
        sq_summed = sem("sq_summed")
        root_done = sem("root_done")
        z_done = sem("z_done")
        op_hi = sem("op_hi")
        op_lo = sem("op_lo")
        q_nope = sem("q_nope")
        qk_done = sem("qk_done")
        max_done = sem("max_done")
        exp_done = sem("exp_done")
        prob_done = sem("prob_done")
        turned = sem("turned")
        turned_copied = sem("turned_copied")
        pv_done = sem("pv_done")
        dve_step = sem("dve_step")
        gate_tanh = sem("gate_tanh")
        out_ready = sem("out_ready")
        pool_step = sem("pool_step")
        conv_sq = sem("conv_sq")
        conv_v = sem("conv_v")
        conv_t = sem("conv_t")
        conv_s = sem("conv_s")
        q_ready = sem("q_ready")
        cond_tanh = sem("cond_tanh")
        cond_done = sem("cond_done")
        conv_a = sem("conv_a")
        fin_z = sem("fin_z")
        stored = sem("stored")

        block = stack.enter_context(nc.Block())

        def parts(kind, slot):
            if kind in ("plain", "short"):
                n = SLOT if kind == "plain" else SLOT // 4
                return [(Wraw[:, slot, 0:n], Whi[:, slot, 0:n], Wlo[:, slot, 0:n])]
            if kind == "keys":
                raw = Wraw[:, slot, 0:4 * P].rearrange("p (k h e d) -> p k h e d", k=2, h=2, e=2)
                both = [w[:, slot, 0:4 * P].rearrange("p (k e h d) -> p k e h d", k=2, h=2, e=2) for w in (Whi, Wlo)]
                return [(raw[:, :, :, e, :], both[0][:, :, e, :, :], both[1][:, :, e, :, :]) for e in range(2)]
            if kind == "rope":
                groups, raw_w, packed_w, at = DT, ROPE, 2 * ROPE, 0
            else:
                groups, raw_w, packed_w, at = 6, NOPE + ROPE, P, NOPE
            src = Wraw[:, slot, 0:groups * raw_w].rearrange("p (g n) -> p g n", g=groups)
            dst = [w[:, slot, 0:groups * packed_w].rearrange("p (g n) -> p g n", g=groups) for w in (Whi, Wlo)]
            res = [(src, dst[0][:, :, 0:raw_w], dst[1][:, :, 0:raw_w])]
            for g in range(2):
                for b in range(2):
                    s0, d0 = at + 16 * g + 8 * (1 - b), raw_w + 16 * g + 8 * b
                    res.append((src[:, :, s0:s0 + 8], dst[0][:, :, d0:d0 + 8], dst[1][:, :, d0:d0 + 8]))
            return res

        def split_hi(act, at, kind, row=None):
            slot, n = at.chunk.n % SLOTS, at.chunk.n
            if at.chunk.var is None:
                act.wait_ge(raw_in[slot], 16 * (n // SLOTS + 1))
            else:
                act.wait_ge(raw_in[slot], at.chunk.var * (16 * at.chunk.step // SLOTS) + 16 * (n // SLOTS + 1))
            if at.tiles.n:
                act.wait_ge(tile_done, at.tiles.now())
            if row is not None and (at.group.n or row > 1):
                act.wait_ge(mod_used, at.group.now() * GROUP + (row - 1))
            for raw, hi, _ in parts(kind, slot):
                last = act.activation(hi, raw, ACT.Copy)
            last.then_inc(hi_done, 1)
            at.chunk.next()

        def split_lo(eng, mine, at, kind):
            slot = at.chunk.n % SLOTS
            if slot % 2 == mine:
                eng.wait_ge(hi_done, at.chunk.now() + 1)
                for raw, hi, lo in parts(kind, slot):
                    last = eng.tensor_tensor(lo, raw, hi.bitcast(F32), ALU.subtract)
                last.then_inc(lo_done[slot], 1)
            at.chunk.next()

        NS = [2, 1]
        half = [slice(s * SEQ, (s + 1) * SEQ) for s in range(2)]

        def by_stream(ap, l):
            return ap.rearrange("p (s n) -> p s n", s=2)[:, 0:NS[l], :]

        def units_of(l):
            return [(h, s * SEQ + q * P, 2 * s, 4 - 2 * s)
                    for h in range(2) for s in range(NS[l]) for q in range(2)]

        def stat_root(l, k):
            return 5 * l + k + 1

        @block.sync
        def _(sp):
            at = Place()
            sp.dma_start(G[:, 0:4, :].rearrange("p (t h) n -> p t (h n)", t=2),
                         x[0].rearrange("(t p) d -> p t d", p=P)).then_inc(x_in, 16)
            sp.dma_start(G[:, 4:8, :].rearrange("p (t h) n -> p t (h n)", t=2),
                         ctx_in[0].rearrange("(t p) d -> p t d", p=P)).then_inc(x_in, 16)

            def load(w, row0, k, col, width):
                slot, n = at.chunk.n % SLOTS, at.chunk.n
                if at.chunk.var is not None:
                    sp.wait_ge(lo_done[slot], at.chunk.var * (at.chunk.step // SLOTS) + n // SLOTS)
                    sp.sem_inc(slot_free, 1)
                elif n >= SLOTS:
                    sp.wait_ge(lo_done[slot], n // SLOTS)
                sp.dma_start(Wraw[:, slot, 0:k * width].rearrange("p (k n) -> p k n", k=k),
                             w[row0:row0 + k * P, bass.ds(col, width)].rearrange(
                                 "(k p) n -> p k n", p=P)).then_inc(raw_in[slot], 16)
                at.chunk.next()

            def mod(l, n):
                load(w_mod[l], 0, DT, n * CW, CW)

            for n in range(GROUP):
                mod(0, n)
            with at.loop(sp, 3, chunks=GROUP) as i:
                for n in range(GROUP):
                    load(w_mod[0], 0, DT, i * (GROUP * CW) + (GROUP + n) * CW, CW)
            for l in range(DEPTH):
                wi = w_in[l]
                cols = [KV0, KV0 + CW, ROPE0, 0, CW, 2 * CW]
                cols += [c0 + j * CW for c0 in (GLU0 + CH, GLU0, SC0 + CH, SC0 + 2 * CH, SC0) for j in range(2)]
                for n, col in enumerate(cols):
                    if l == 0:
                        mod(0, 16 + n)
                    load(wi, 0, DT, col, ROPE if col == ROPE0 else CW)

                def pair(p):
                    n = 2 * (NOPE + ROPE)
                    load(w_kv_b[l], 0, 2, p * (2 * P), 2 * P)
                    load(w_q_b[l], 0, 3, p * n, n)
                    for j in range(2):
                        load(wi, 0, DT, p * (2 * CW) + (GATE0 + j * CW), CW)

                with at.loop(sp, PAIRS - 1, chunks=4) as i:
                    pair(i)
                pair(PAIRS - 1)
                for j in range(4):
                    load(w_mla_o[l], 0, 4, j * 2 * CW, 2 * CW)
                with at.loop(sp, 4, chunks=12 if l == 0 else 8) as i:
                    for j in range(2):
                        for b in range(2):
                            if l == 0:
                                load(w_mod[0], 0, DT, i * (4 * CW) + (32 + 2 * j + b) * CW, CW)
                            load(wi, 0, DT, i * (2 * CW) + (GATE0 + (b + 1) * D + j * CW), CW)
                        for w in (w_conv_o, w_sc_o):
                            load(w[l], 0, 2, i * (2 * CW) + j * CW, CW)
                with at.loop(sp, 2, chunks=4) as i:
                    for j in range(4):
                        load(w_o[l], 0, DT, i * (4 * CW) + j * CW, CW)
                if l == 0:
                    for n in range(GROUP):
                        mod(1, n)
                g0 = 0
                for n in FF_GROUPS:
                    with at.loop(sp, n // 2, chunks=8 if l == 0 else 4) as i:
                        for b, w in enumerate((w_ff1, w_ff3)):
                            for j in range(2):
                                if l == 0:
                                    load(w_mod[1], 0, DT,
                                         i * (GROUP * CW) + (GROUP + 2 * g0 + 2 * b + j) * CW, CW)
                                load(w[l], 0, DT, i * (2 * CW) + (g0 + j) * P, CW)
                    with at.loop(sp, 2, chunks=4) as i:
                        for j in range(4):
                            load(w_ff2[l], g0 * P, n, i * (4 * CW) + j * CW, CW)
                    g0 += n
            for t in range(2):
                sp.wait_ge(out_ready, 2 * (t + 1))
                sp.dma_start(out[0, t * P:(t + 1) * P, :].rearrange("p (h n) -> p h n", h=2),
                             X[:, 2 * t:2 * t + 2, :]).then_inc(stored, 16)
            sp.wait_ge(stored, 32)

        @block.gpsimd
        def _(pool):
            at = Place()
            step = Tally()

            def mark(ins):
                ins.then_inc(pool_step, 1)
                return step.next()

            mark(pool.memset(IDN[:, :], 0.0))
            v = mark(pool.memset(SEL[:, :], 0.0))
            pool.memset(ONES[:, :], 1.0).then_inc(consts, 1)
            pool.wait_ge(pool_step, v)
            pool.affine_select(out=IDN[:, :], in_=IDN[:, :], compare_op=ALU.not_equal, fill=1.0,
                               base=0, pattern=[[-1, P]], channel_multiplier=1).then_inc(consts, 1)
            for base in (0, -2):
                v = mark(pool.affine_select(out=SEL[:, :], in_=SEL[:, :], compare_op=ALU.not_equal, fill=1.0,
                                            base=base, pattern=[[-1, 2]], channel_multiplier=1))
                pool.wait_ge(pool_step, v)
            pool.memset(U[:, :, :, :].rearrange("p a b c -> p (a b c)"), 0.0).then_inc(consts, 1)
            pool.memset(C[:, :, :, :].rearrange("p a b c -> p (a b c)"), 0.0).then_inc(consts, 1)

            def clear_sum(roots):
                if roots:
                    pool.wait_ge(root_done, roots)
                v = mark(pool.memset(SUM[:, :], 0.0))
                pool.wait_ge(pool_step, v)

            def add_square(n):
                slot = at.square.n % 2
                if at.square.n:
                    pool.wait_ge(sq_summed, at.square.now())
                pool.wait_ge(sq_done, at.square.now() + 1)
                pool.tensor_tensor(SUM[:, 0:n], SUM[:, 0:n], SQ[:, slot, 0:n], ALU.add).then_inc(sq_summed, 1)
                at.square.next()

            def look(kind="plain"):
                split_lo(pool, 0, at, kind)

            look()
            look()
            clear_sum(0)
            for _ in range(DT):
                add_square(T)
            for _ in range(GROUP):
                look()
            with at.loop(pool, 3, chunks=GROUP):
                for _ in range(GROUP):
                    look()
            for l in range(DEPTH):
                TQ = NS[l] * SEQ
                nxt = ahead(projection_kinds(l), PAIR_KINDS[:2])

                def step_in():
                    for _ in range(2 if l == 0 else 1):
                        look(next(nxt))

                clear_sum(stat_root(l, 0))
                for _ in range(2):
                    step_in()
                    add_square(T)
                step_in()
                clear_sum(stat_root(l, 1))
                for _ in range(3):
                    step_in()
                    add_square(TQ)
                for _ in range(10):
                    step_in()
                with at.loop(pool, PAIRS - 1, chunks=4):
                    for kind in ahead(PAIR_KINDS, PAIR_KINDS[:2]):
                        look(kind)
                for _ in range(8):
                    look()
                with at.loop(pool, 4, chunks=12 if l == 0 else 8):
                    for kind in ahead(branch_kinds(l), ["plain"] * 2):
                        look(kind)
                clear_sum(stat_root(l, 2))
                with at.loop(pool, 2, chunks=4, squares=4):
                    for _ in range(4):
                        look()
                        add_square(TQ)
                if l == 0:
                    for _ in range(GROUP):
                        look()
                for g, n in enumerate(FF_GROUPS):
                    last = g == len(FF_GROUPS) - 1
                    with at.loop(pool, n // 2, chunks=8 if l == 0 else 4):
                        for _ in range(8 if l == 0 else 4):
                            look()
                    if last:
                        clear_sum(stat_root(l, 4))
                    if last and l == DEPTH - 1:
                        for j in range(8):
                            if j < 6:
                                look()
                            add_square(TQ)
                    else:
                        with at.loop(pool, 2, chunks=4, squares=4 * last):
                            for _ in range(4):
                                look()
                                if last:
                                    add_square(TQ)

        @block.scalar
        def _(act):
            at = Place()

            for row, v in ((CVEC, c[0]), (CVEC + DT, c_ctx), (FING, final_g)):
                act.dma_start(PST[row:row + DT, 0, 3 * P:4 * P],
                              v.rearrange("(t p) -> t p", p=P)).then_inc(shared_in, 16)
            act.dma_start(PST[0:2 * NMOD * DT, 0, 2 * P:3 * P],
                          b_mod.rearrange("l (t p) -> (l t) p", p=P)).then_inc(vec_in, 16)
            for row, v in ((LN1, ln1_g), (LN2, ln2_g), (QG, q_a_norm_g), (KVG, kv_a_norm_g),
                           (CB, conv_dw_b), (LNG, conv_ln_g), (LNB, conv_ln_b)):
                n = v.shape[1] // P
                act.dma_start(PST[row:row + n, 0, 0:2 * P].rearrange("t (l p) -> t l p", l=2),
                              v.rearrange("l (t p) -> t l p", p=P)).then_inc(vec_in, 16)
            for row, v in ((CDW, conv_dw), (SCW, sc_dw)):
                n = v.shape[1] * v.shape[2] // P
                act.dma_start(PST[row:row + n, 0, 0:2 * P].rearrange("t (l p) -> t l p", l=2),
                              v.rearrange("l w (t p) -> (w t) l p", p=P)).then_inc(vec_in, 16)
            act.dma_start(TAB[:, :], rope).then_inc(vec_in, 16)

            def look(kind="plain", row=None):
                split_hi(act, at, kind, row)

            def copy_out(dst, n=T, func=ACT.Copy, scale=1.0, m=P):
                t = at.tile()
                act.wait_ge(tile_done, t.done)
                act.activation(dst, banks[t.bank][0:m, 0:n], func, scale=scale).then_inc(drained[t.bank], 1)
                return t

            def square(src, n):
                slot = at.square.n % 2
                if at.square.n >= 2:
                    act.wait_ge(sq_summed, at.square.now() - 1)
                act.activation(SQ[:, slot, 0:n], src, ACT.Square).then_inc(sq_done, 1)
                at.square.next()

            def root(n, width):
                t = at.tile()
                act.wait_ge(tile_done, t.done)
                act.activation(ROOT[:, 0:n], banks[t.bank][:, 0:n], ACT.Sqrt, bias=EPS,
                               scale=1.0 / width).then_inc(root_done, 1)

            def mod_row():
                group = at.group.now()
                act.wait_ge(mod_used, group * GROUP + GROUP)
                if at.group.n:
                    act.wait_ge(mod_cols, group)
                act.activation(ROW, S[0][0:4, :], ACT.Copy).then_inc(mod_rows, 1)
                at.group.next()

            def operand(dst, src, z=True, scale=1.0):
                if z:
                    at.z += 1
                    act.wait_ge(z_done, at.z)
                act.activation(dst, src, ACT.Copy, scale=scale).then_inc(op_hi, 1)
                at.operand.next()

            def normed_h(l, mod, n_streams):
                for k in range(DT):
                    at.z += 1
                    act.wait_ge(z_done, at.z)
                    for s in range(n_streams):
                        last = act.activation(Hhi[:, k, half[s]], Z[:, k % 2, half[s]], ACT.Identity,
                                              bias=MOD[:, l, mod * DT + k, s:s + 1])
                    last.then_inc(op_hi, 1)
                    at.operand.next()

            t = at.tile()
            act.wait_ge(drained[t.bank], t.drained)
            act.activation(CTH[:, :], PAR[:, 3, CVEC:CVEC + 2 * DT], ACT.Tanh, scale=0.5).then_inc(cond_tanh, 1)
            look()
            look()
            for k in range(DT):
                t = copy_out(X[:, k, :])
                act.wait_ge(drained[t.bank], t.drained)
                square(X[:, k, :], T)
            at.tile()

            for row in range(GROUP):
                look(row=row)
            mod_row()
            root(T, D)
            with at.loop(act, 3, chunks=GROUP, groups=1):
                for row in range(GROUP):
                    look(row=row)
                mod_row()
            for l in range(DEPTH):
                TQ = NS[l] * SEQ
                normed_h(l, 0, 2)
                nxt = ahead(projection_kinds(l), PAIR_KINDS[:2])
                seen = [0]

                def step_in():
                    look(next(nxt))
                    if l == 0:
                        look(next(nxt))
                        seen[0] += 1
                        if seen[0] % GROUP == 0:
                            mod_row()

                for j in range(2):
                    step_in()
                    t = at.tile()
                    act.wait_ge(tile_done, t.done)
                    square(banks[t.bank][:, :], T)
                step_in()
                at.tile()
                root(T, KVL)
                for k in range(2):
                    operand(Uhi[:, CT0 + k, :], Z[:, k % 2, :])
                for j in range(3):
                    step_in()
                    t = at.tile()
                    act.wait_ge(tile_done, t.done)
                    square(banks[t.bank][:, 0:TQ], TQ)
                for j in range(2):
                    step_in()
                    copy_out(TG[:, j, 0:TQ], TQ, ACT.Tanh, 0.5)
                root(TQ, QL)
                for k in range(3):
                    operand(Uhi[:, QT + k, 0:TQ], Z[:, k % 2, 0:TQ])
                glu = []
                for j in range(2):
                    step_in()
                    glu.append(at.tile())
                for j in range(2):
                    step_in()
                    act.wait_ge(drained[glu[j].bank], glu[j].drained)
                    copy_out(TG[:, j, 0:TQ], TQ)
                for j in range(2):
                    step_in()
                    at.tile()
                for j in range(2):
                    step_in()
                    copy_out(BG[:, j, 0:TQ], TQ)

                units = units_of(l)

                def pair(p, after):
                    nxt = ahead(PAIR_KINDS, after)
                    look(next(nxt))
                    t = at.tile()
                    act.wait_ge(tile_done, t.done)
                    for h in range(2):
                        last = act.activation(Kb[0:NOPE, h, :], banks[t.bank][h * NOPE:(h + 1) * NOPE, :], ACT.Copy)
                    last.then_inc(drained[t.bank], 1)
                    copy_out(V[:, :, :].rearrange("p t n -> p (t n)"))
                    look(next(nxt))
                    for h in range(2):
                        t = at.tile()
                        act.wait_ge(tile_done, t.done)
                        act.activation(Qb[0:NOPE, h, 0:TQ], banks[t.bank][0:NOPE, 0:TQ], ACT.Copy,
                                       scale=SCALE).then_inc(q_nope, 1)

                    def exps(u):
                        _, _, _, kt = units[u]
                        act.wait_ge(max_done, at.unit.now() + 1)
                        if u >= 2:
                            act.wait_ge(turned, at.unit.now() - 1)
                        act.activation(PR[:, u % 2, 0:kt * P], S[u % 2][:, 0:kt * P], ACT.Exp,
                                       bias=NM[:, u % 2:u % 2 + 1],
                                       accum_out=RS[:, u % 2:u % 2 + 1]).then_inc(exp_done, 1)
                        at.unit.next()

                    def copy_turned(u):
                        kt = units[u][3]
                        done = at.unit.now() - (n_done[0] - u) + 1
                        act.wait_ge(turned, done)
                        if u >= 2:
                            act.wait_ge(pv_done, done - 2)
                        act.activation(PTs[:, u % 2, 0:kt * P], PT[:, 0:kt * P], ACT.Copy).then_inc(turned_copied, 1)

                    n_done = [0]

                    def exps_(u):
                        exps(u)
                        n_done[0] += 1

                    exps_(0)
                    exps_(1)
                    look(next(nxt))
                    look(next(nxt))
                    copy_out(G[:, p * 2, 0:TQ], TQ, ACT.Tanh, 0.5)
                    for u in range(2, len(units)):
                        copy_turned(u - 2)
                        exps_(u)
                    copy_turned(len(units) - 2)
                    copy_turned(len(units) - 1)
                    copy_out(G[:, p * 2 + 1, 0:TQ], TQ, ACT.Tanh, 0.5)
                    act.wait_ge(pv_done, at.unit.now())
                    act.activation(Uhi[:, p + AT0, 0:TQ], PV[:, 0:TQ], ACT.Copy).then_inc(op_hi, 1)
                    at.operand.next()

                with at.loop(act, PAIRS - 1, chunks=4, tiles=6, units=len(units), operands=1) as i:
                    pair(i, PAIR_KINDS[:2])
                pair(PAIRS - 1, ["plain"] * 2)

                look()
                look()
                act.wait_ge(conv_a, l + 1)
                for j in range(2):
                    operand(Uhi[:, SO0 + j, 0:TQ], BG[:, j, 0:TQ], z=False)
                at.tile()
                at.tile()
                mean = at.tile()
                act.wait_ge(drained[mean.bank], mean.drained)
                for j in range(2):
                    last = act.activation(SQ[:, j, 0:TQ], ACC[:, j, 0:TQ], ACT.Square)
                last.then_inc(conv_sq, 1)
                at.tile()
                at.tile()
                root(TQ, CH)
                look()
                look()
                act.wait_ge(conv_v, l + 1)
                for j in range(2):
                    last = act.activation(TG[:, j, 0:TQ], ACC[:, j, 0:TQ], ACT.Tanh, scale=0.5)
                last.then_inc(conv_t, 1)
                act.wait_ge(conv_s, l + 1)
                for j in range(2):
                    operand(Uhi[:, CO0 + j, 0:TQ], Z[:, j, 0:TQ], z=False, scale=0.5)
                for _ in range(4):
                    at.tile()

                with at.loop(act, 4, chunks=12 if l == 0 else 8, tiles=8, groups=1 if l == 0 else 0):
                    nxt = ahead(branch_kinds(l), ["plain"] * 2)
                    free = [(2 + j, at.uses[2 + j].now()) for j in range(2)]
                    for m in range(2):
                        for j in range(2):
                            look(next(nxt))
                            if l == 0:
                                look(next(nxt))
                                if m == 1 and j == 1:
                                    mod_row()
                            act.wait_ge(drained[free[j][0]], free[j][1])
                            copy_out(TG[:, j, 0:TQ], TQ, ACT.Tanh, 0.5)
                        look(next(nxt))
                        look(next(nxt))
                        free = [(t.bank, t.drained) for t in (at.tile(), at.tile())]
                summed = [u.now() for u in at.uses]
                for b in range(4):
                    act.wait_ge(drained[b], summed[b])
                for k in range(DT):
                    operand(Hhi[:, k, 0:TQ], G[:, k, 0:TQ], z=False, scale=0.5)

                def residual_squares(m):
                    t = at.tile()
                    act.wait_ge(drained[t.bank], t.drained)
                    square(X[:, m, 0:TQ], TQ)

                with at.loop(act, 2, chunks=4, tiles=4, squares=4) as i:
                    for j in range(4):
                        look()
                        residual_squares(i * 4 + j)
                root(TQ, D)
                if l == 0:
                    for row in range(GROUP):
                        look(row=row)
                    mod_row()
                normed_h(l, 3, NS[l])
                h0 = 0
                for g, n in enumerate(FF_GROUPS):
                    last = g == len(FF_GROUPS) - 1
                    mixed = 1 if l == 0 else 0
                    with at.loop(act, n // 2, chunks=4 + 4 * mixed, tiles=4, operands=2, groups=mixed) as i:
                        for j in range(2):
                            for _ in range(1 + mixed):
                                look()
                            t = at.tile()
                            act.wait_ge(tile_done, t.done)
                            act.activation(TG[:, j, 0:TQ], banks[t.bank][:, 0:TQ], ACT.Tanh,
                                           scale=0.5).then_inc(gate_tanh, 1)
                        for j in range(2):
                            for _ in range(1 + mixed):
                                look()
                            if mixed and j == 1:
                                mod_row()
                            t = at.tile()
                            act.wait_ge(drained[t.bank], t.drained)
                            act.activation(Uhi[:, i * 2 + j, 0:TQ], PR[:, j, 0:TQ],
                                           ACT.Copy).then_inc(op_hi, 1)
                            at.operand.next()
                    if last and l == DEPTH - 1:
                        for j in range(8):
                            if j < 6:
                                look()
                            residual_squares(j)
                    else:
                        with at.loop(act, 2, chunks=4, tiles=4, squares=4 * last) as i:
                            for j in range(4):
                                look()
                                if last:
                                    residual_squares(i * 4 + j)
                                else:
                                    at.tile()
                root(SEQ if l == DEPTH - 1 else T, D)
            act.wait_ge(fin_z, DT)
            for k in range(4):
                t = at.tile()
                act.wait_ge(tile_done, t.done)
                act.activation(X[:, k, :], banks[t.bank][:, :], ACT.Copy).then_inc(out_ready, 1)

        @block.vector
        def _(dve):
            at = Place()
            step = Tally()
            add, mult, sub = ALU.add, ALU.mult, ALU.subtract

            def mark(ins):
                ins.then_inc(dve_step, 1)
                return step.next()

            def after_all():
                dve.wait_ge(dve_step, step.now())

            def settle():
                after_all()
                if at.operand.n:
                    dve.wait_ge(op_lo, at.operand.now())

            def look(kind="plain"):
                split_lo(dve, 1, at, kind)

            def full():
                t = at.tile()
                dve.wait_ge(tile_done, t.done)
                return t

            def through(t):
                dve.wait_ge(drained[t.bank], t.drained)

            def mod_add(l, first):
                dve.wait_ge(mod_cols, at.group.next())
                for s in range(2):
                    last = dve.tensor_tensor(
                        MOD[:, l, bass.ds(first, GROUP), s],
                        S[1][:, 0:2 * GROUP].rearrange("p (f s) -> p f s", s=2)[:, :, s],
                        PAR[:, 2, bass.ds(first + l * NMOD * DT, GROUP)], add)
                last.then_inc(mod_done, 1)

            def take_root(n, roots):
                t = at.tile()
                settle()
                dve.wait_ge(root_done, roots)
                dve.reciprocal(RSTD[:, 0:n], ROOT[:, 0:n]).then_inc(drained[t.bank], 1)
                through(t)

            def low(dst, src, hi, scale=None, shift=None):
                dve.wait_ge(op_hi, at.operand.now() + 1)
                if scale is not None:
                    ins = [dve.scalar_tensor_tensor(dst, src, scale, hi.bitcast(F32), mult, sub)]
                elif shift is not None:
                    ins = [dve.scalar_tensor_tensor(dst[:, h], src[:, h], b, hi[:, h].bitcast(F32), add, sub)
                           for h, b in shift]
                else:
                    ins = [dve.tensor_tensor(dst, src, hi.bitcast(F32), sub)]
                ins[-1].then_inc(op_lo, 1)
                at.operand.next()

            def normed_h(l, mod, gain, n_streams):
                settle()
                for s in range(n_streams):
                    mark(dve.scalar_tensor_tensor(AV[:, :, s], MOD[:, l, (mod + 1) * DT:(mod + 2) * DT, s], 1.0,
                                                  PAR[:, l, gain:gain + DT], add, mult))
                after_all()

                def low_part(k):
                    low(Hlo[:, k, :], Z[:, k % 2, :], Hhi[:, k, :],
                        shift=[(half[s], MOD[:, l, mod * DT + k, s:s + 1]) for s in range(n_streams)])

                for k in range(DT):
                    settle()
                    for s in range(n_streams):
                        last = dve.scalar_tensor_tensor(Z[:, k % 2, half[s]], X[:, k, half[s]], AV[:, k, s:s + 1],
                                                        RSTD[:, half[s]], mult, mult)
                    last.then_inc(z_done, 1)
                    if k:
                        low_part(k - 1)
                low_part(DT - 1)

            def normed(l, n, tiles, raw0, to, gain):
                def low_part(k):
                    low(Ulo[:, to + k, 0:n], Z[:, k % 2, 0:n], Uhi[:, to + k, 0:n])

                for k in range(tiles):
                    settle()
                    dve.scalar_tensor_tensor(Z[:, k % 2, 0:n], G[:, raw0 + k, 0:n],
                                             PAR[:, l, gain + k:gain + k + 1], RSTD[:, 0:n],
                                             mult, mult).then_inc(z_done, 1)
                    if k:
                        low_part(k - 1)
                low_part(tiles - 1)

            def keep_raw(k, n):
                t = full()
                dve.wait_ge(sq_done, at.square.next())
                dve.tensor_copy(G[:, k, 0:n], banks[t.bank][:, 0:n]).then_inc(drained[t.bank], 1)

            t = full()
            dve.tensor_copy(PAR[:, 3, 0:CVEC + 2 * DT], banks[t.bank][:, 0:CVEC + 2 * DT]).then_inc(
                drained[t.bank], 1)
            dve.wait_ge(cond_tanh, 1)
            CSf = CS[:, :, :].rearrange("p s k -> p (s k)")
            mark(dve.scalar_tensor_tensor(CSf, CTH[:, :], 1.0, PAR[:, 3, CVEC:CVEC + 2 * DT], add, mult))
            after_all()
            cv = [CV[:, :, 2 * j:2 * j + 2].rearrange("p k s -> p s k") for j in range(2)]
            mark(dve.tensor_scalar(cv[0], CS[:, :, :], 0.5, None, mult))
            after_all()
            dve.scalar_tensor_tensor(cv[1], CS[:, :, :], 0.5, cv[0].bitcast(F32), mult, sub).then_inc(cond_done, 1)
            look()
            look()
            for _ in range(DT):
                at.tile()
                at.square.next()
            t = full()
            for b, n in enumerate((ROWS, ROWS, 2 * NMOD * DT)):
                last = dve.tensor_copy(PAR[:, b, 0:n], banks[t.bank][:, b * P:b * P + n])
            last.then_inc(drained[t.bank], 1)
            through(t)
            for _ in range(GROUP):
                look()
            mod_add(0, 0)
            take_root(T, stat_root(0, 0))
            with at.loop(dve, 3, chunks=GROUP, groups=1) as i:
                for _ in range(GROUP):
                    look()
                mod_add(0, i * GROUP + GROUP)
            dve.wait_ge(consts, 4)
            for l in range(DEPTH):
                TQ = NS[l] * SEQ
                dve.wait_ge(mod_done, at.group.n)
                normed_h(l, 0, LN1, 2)
                nxt = ahead(projection_kinds(l), PAIR_KINDS[:2])
                seen = [0]

                def step_in():
                    for _ in range(2 if l == 0 else 1):
                        look(next(nxt))

                def step_out():
                    seen[0] += 1
                    if l == 0 and seen[0] % GROUP == 0:
                        mod_add(0, 16 + seen[0] - GROUP)

                for j in range(2):
                    step_in()
                    keep_raw(j, T)
                    step_out()
                step_in()
                settle()
                t = full()
                mark(dve.tensor_tensor(Z[64:96, 0, :], banks[t.bank][0:32, :], TAB[0:32, :], mult))
                dve.tensor_tensor(Z[64:96, 1, :], banks[t.bank][32:64, :], TAB[32:64, :], mult).then_inc(
                    drained[t.bank], 1)
                after_all()
                through(t)
                for h in range(2):
                    mark(dve.tensor_tensor(Kb[64:96, h, :], Z[64:96, 0, :], Z[64:96, 1, :], add))
                take_root(T, stat_root(l, 1))
                normed(l, T, 2, 0, CT0, KVG)
                step_out()
                for j in range(3):
                    step_in()
                    keep_raw(2 + j, TQ)
                    step_out()
                tanh_g = []
                for j in range(2):
                    step_in()
                    tanh_g.append(at.tile())
                    step_out()
                take_root(TQ, stat_root(l, 2))
                normed(l, TQ, 3, 2, QT, QG)
                for j in range(2):
                    step_in()
                    t = full()
                    dve.wait_ge(drained[tanh_g[j].bank], tanh_g[j].drained)
                    dve.scalar_tensor_tensor(U[:, j, 0:NS[l], PAD:PAD + SEQ], by_stream(TG[:, j, :], l), 1.0,
                                             by_stream(banks[t.bank][:, :], l), add, mult).then_inc(
                                                 drained[t.bank], 1)
                    step_out()
                through(t)

                def tap(w, start):
                    for j in range(2):
                        dve.wait_ge(dve_step, step.now() - 1)
                        mark(dve.scalar_tensor_tensor(
                            by_stream(ACC[:, j, :], l), U[:, j, 0:NS[l], bass.ds(start, SEQ)],
                            PAR[:, l, bass.ds(w + j, 1)], by_stream(ACC[:, j, :], l), mult, add))

                for j in range(2):
                    mark(dve.tensor_scalar(by_stream(ACC[:, j, :], l), U[:, j, 0:NS[l], 0:SEQ],
                                           PAR[:, l, CDW + j:CDW + j + 1], None, mult))
                gates = []
                for j in range(2):
                    step_in()
                    gates.append(at.tile())
                    tap(CDW + 2 * (j + 1), j + 1)
                    step_out()
                for j in range(2):
                    step_in()
                    t = full()
                    dve.wait_ge(drained[gates[j].bank], gates[j].drained)
                    dve.tensor_tensor(C[:, j, 0:NS[l], 1:1 + SEQ], by_stream(TG[:, j, :], l),
                                      by_stream(banks[t.bank][:, :], l), mult).then_inc(drained[t.bank], 1)
                    step_out()
                through(t)
                for w in range(SC_TAPS):
                    for j in range(2):
                        wt = PAR[:, l, SCW + 2 * w + j:SCW + 2 * w + j + 1]
                        src, acc = C[:, j, 0:NS[l], w:w + SEQ], by_stream(Z[:, j, :], l)
                        if w == 0:
                            mark(dve.tensor_scalar(acc, src, wt, None, mult))
                        else:
                            dve.wait_ge(dve_step, step.now() - 1)
                            mark(dve.scalar_tensor_tensor(acc, src, wt, acc, mult, add))
                for j in range(2):
                    step_in()
                    t = at.tile()
                    dve.wait_ge(drained[t.bank], t.drained)
                    dve.wait_ge(dve_step, step.now() - 1 + j)
                    mark(dve.tensor_tensor(BG[:, j, 0:TQ], BG[:, j, 0:TQ], Z[:, j, 0:TQ], mult))
                    step_out()

                units = units_of(l)

                def pair(p, after):
                    nxt = ahead(PAIR_KINDS, after)
                    look(next(nxt))
                    look(next(nxt))
                    at.tile()
                    at.tile()
                    after_all()
                    for h in range(2):
                        t = full()
                        bank = banks[t.bank]
                        if h:
                            dve.wait_ge(q_ready, at.heads.now())
                        mark(dve.scalar_tensor_tensor(Z[64:96, 0, 0:TQ], bank[64:96, 0:TQ], SCALE,
                                                      TAB[64:96, 0:TQ], mult, mult))
                        dve.wait_ge(q_nope, at.heads.next())
                        dve.scalar_tensor_tensor(Z[64:96, 1, 0:TQ], bank[96:128, 0:TQ], SCALE,
                                                 TAB[96:128, 0:TQ], mult, mult).then_inc(drained[t.bank], 1)
                        after_all()
                        through(t)
                        dve.tensor_tensor(Qb[64:96, h, 0:TQ], Z[64:96, 0, 0:TQ], Z[64:96, 1, 0:TQ],
                                          add).then_inc(q_ready, 1)
                    taps = iter(range(TAPS_BEFORE, TAPS_BEFORE + TAPS_PER_PAIR))

                    def do_taps(n):
                        for w in [next(taps) for _ in range(n)]:
                            tap(p * (2 * TAPS_PER_PAIR) + (CDW + 2 * w), p * TAPS_PER_PAIR + w)

                    do_taps(1)
                    base = at.unit.n

                    def unit(k):
                        return at.unit.now() - (at.unit.n - base) + k

                    def row_max(u):
                        kt = units[u][3]
                        dve.wait_ge(qk_done, unit(u + 1))
                        dve.tensor_reduce(NM[:, u % 2:u % 2 + 1], S[u % 2][:, 0:kt * P], AX.X, ALU.max,
                                          negate=True).then_inc(max_done, 1)

                    def normalise(u):
                        kt = units[u][3]
                        dve.wait_ge(exp_done, unit(u + 1))
                        mark(dve.reciprocal(RR[:, u % 2:u % 2 + 1], RS[:, u % 2:u % 2 + 1]))
                        after_all()
                        dve.tensor_scalar(PR[:, u % 2, 0:kt * P], PR[:, u % 2, 0:kt * P],
                                          RR[:, u % 2:u % 2 + 1], None, mult).then_inc(prob_done, 1)

                    row_max(0)
                    row_max(1)
                    normalise(0)
                    look(next(nxt))
                    look(next(nxt))
                    per = (TAPS_PER_PAIR - 1) // (len(units) - 2)
                    for u in range(2, len(units)):
                        row_max(u)
                        normalise(u - 1)
                        do_taps(per)
                    normalise(len(units) - 1)
                    for _ in units:
                        at.unit.next()
                    at.tile()
                    at.tile()
                    low(Ulo[:, p + AT0, 0:TQ], PV[:, 0:TQ], Uhi[:, p + AT0, 0:TQ])

                steps = 2 + 2 * TAPS_PER_PAIR + len(units)
                with at.loop(dve, PAIRS - 1, chunks=4, tiles=6, units=len(units), operands=1, heads=2,
                             extra=[(step, steps)]) as i:
                    pair(i, PAIR_KINDS[:2])
                pair(PAIRS - 1, ["plain"] * 2)

                def attended(m):
                    t = full()
                    dve.scalar_tensor_tensor(G[:, m, 0:TQ], G[:, m, 0:TQ], 1.0, banks[t.bank][:, 0:TQ],
                                             add, mult).then_inc(drained[t.bank], 1)

                look()
                look()
                after_all()
                for j in range(2):
                    last = dve.tensor_scalar(ACC[:, j, 0:TQ], ACC[:, j, 0:TQ], 0.5,
                                             PAR[:, l, CB + j:CB + j + 1], mult, add)
                last.then_inc(conv_a, 1)
                for j in range(2):
                    low(Ulo[:, SO0 + j, 0:TQ], BG[:, j, 0:TQ], Uhi[:, SO0 + j, 0:TQ])
                attended(0)
                attended(1)
                t = full()
                dve.wait_ge(conv_a, l + 1)
                for j in range(2):
                    last = dve.scalar_tensor_tensor(ACC[:, j, 0:TQ], banks[t.bank][:, 0:TQ], -1.0 / CH,
                                                    ACC[:, j, 0:TQ], mult, add)
                last.then_inc(drained[t.bank], 1)
                attended(2)
                attended(3)
                take_root(TQ, stat_root(l, 3))
                look()
                look()
                for j in range(2):
                    mark(dve.tensor_tensor(Z[:, j, 0:TQ], ACC[:, j, 0:TQ], RSTD[:, 0:TQ], mult))
                after_all()
                for j in range(2):
                    last = dve.tensor_scalar(ACC[:, j, 0:TQ], Z[:, j, 0:TQ], PAR[:, l, LNG + j:LNG + j + 1],
                                             PAR[:, l, LNB + j:LNB + j + 1], mult, add)
                last.then_inc(conv_v, 1)
                dve.wait_ge(conv_t, l + 1)
                dve.wait_ge(conv_v, l + 1)
                for j in range(2):
                    last = dve.scalar_tensor_tensor(Z[:, j, 0:TQ], TG[:, j, 0:TQ], 1.0, ACC[:, j, 0:TQ], add, mult)
                last.then_inc(conv_s, 1)
                for j in range(2):
                    low(Ulo[:, CO0 + j, 0:TQ], Z[:, j, 0:TQ], Uhi[:, CO0 + j, 0:TQ], scale=0.5)
                for m in range(4, DT):
                    attended(m)

                settle()
                with at.loop(dve, 4, chunks=12 if l == 0 else 8, tiles=8, groups=1 if l == 0 else 0,
                             extra=[(step, 4)]) as i:
                    nxt = ahead(branch_kinds(l), ["plain"] * 2)
                    free = [(2 + j, at.uses[2 + j].now()) for j in range(2)]
                    for m in range(2):
                        gates = []
                        for j in range(2):
                            for _ in range(2 if l == 0 else 1):
                                look(next(nxt))
                            gates.append(at.tile())
                        for j in range(2):
                            look(next(nxt))
                            t = full()
                            dve.wait_ge(drained[gates[j].bank], gates[j].drained)
                            dve.wait_ge(drained[free[j][0]], free[j][1])
                            mark(dve.scalar_tensor_tensor(Z[:, j, 0:TQ], TG[:, j, 0:TQ], 1.0,
                                                          banks[t.bank][:, 0:TQ], add, mult))
                            after_all()
                            if j:
                                through(t0)
                            dve.tensor_tensor(G[:, i * 2 + m, 0:TQ], G[:, i * 2 + m, 0:TQ], Z[:, j, 0:TQ],
                                              add).then_inc(drained[t.bank], 1)
                            free[j], t0 = (t.bank, t.drained), t
                    if l == 0:
                        mod_add(0, i * GROUP + 32)
                for k in range(DT):
                    low(Hlo[:, k, 0:TQ], G[:, k, 0:TQ], Hhi[:, k, 0:TQ], scale=0.5)

                def residual(m, mod):
                    t = full()
                    for s in range(NS[l]):
                        last = dve.scalar_tensor_tensor(X[:, m, half[s]], banks[t.bank][:, half[s]],
                                                        MOD[:, l, m + mod * DT, s:s + 1], X[:, m, half[s]],
                                                        mult, add)
                    last.then_inc(drained[t.bank], 1)
                    return t

                with at.loop(dve, 2, chunks=4, tiles=4) as i:
                    for j in range(4):
                        look()
                        residual(i * 4 + j, 2)
                at.square.n += DT
                take_root(TQ, stat_root(l, 4))
                if l == 0:
                    for _ in range(GROUP):
                        look()
                    mod_add(1, 0)
                normed_h(l, 3, LN2, NS[l])
                first = 0
                for g, n in enumerate(FF_GROUPS):
                    mixed = 1 if l == 0 else 0
                    with at.loop(dve, n // 2, chunks=4 + 4 * mixed, tiles=4, operands=2, gates=2, groups=mixed) as i:
                        free = [at.uses[2 + j].now() for j in range(2)]
                        for j in range(2):
                            for _ in range(1 + mixed):
                                look()
                            t = full()
                            dve.wait_ge(gate_tanh, at.gates.next())
                            dve.wait_ge(drained[2 + j], free[j])
                            dve.scalar_tensor_tensor(Z[:, j, 0:TQ], TG[:, j, 0:TQ], 1.0, banks[t.bank][:, 0:TQ],
                                                     add, mult).then_inc(drained[t.bank], 1)
                        through(t)
                        dve.wait_ge(op_lo, at.operand.now())
                        for j in range(2):
                            for _ in range(1 + mixed):
                                look()
                            t = full()
                            dve.scalar_tensor_tensor(PR[:, j, 0:TQ], Z[:, j, 0:TQ], 0.5, banks[t.bank][:, 0:TQ],
                                                     mult, mult).then_inc(drained[t.bank], 1)
                            low(Ulo[:, i * 2 + j, 0:TQ], PR[:, j, 0:TQ], Uhi[:, i * 2 + j, 0:TQ])
                        if mixed:
                            mod_add(1, i * GROUP + (GROUP + 2 * first))
                    first += n
                    if g == len(FF_GROUPS) - 1 and l == DEPTH - 1:
                        for j in range(8):
                            if j < 6:
                                look()
                            residual(j, 5)
                    else:
                        with at.loop(dve, 2, chunks=4, tiles=4) as i:
                            for j in range(4):
                                look()
                                residual(i * 4 + j, 5)
                at.square.n += DT
                take_root(T if l == 0 else SEQ, stat_root(l + 1, 0))
            for k in range(DT):
                dve.scalar_tensor_tensor(G[:, k, 0:SEQ], X[:, k, 0:SEQ], PAR[:, 3, FING + k:FING + k + 1],
                                         RSTD[:, 0:SEQ], mult, mult).then_inc(fin_z, 1)

        @block.tensor
        def _(pe):
            at = Place()

            def new_tile():
                t = at.tile()
                if not isinstance(t.before, int) or t.before > 0:
                    pe.wait_ge(drained[t.bank], t.before)
                return t

            def chunk():
                slot, n = at.chunk.n % SLOTS, at.chunk.n
                if at.chunk.var is None:
                    pe.wait_ge(lo_done[slot], n // SLOTS + 1)
                else:
                    pe.wait_ge(lo_done[slot], at.chunk.var * (at.chunk.step // SLOTS) + (n // SLOTS + 1))
                at.chunk.next()
                return slot

            def split_product(dst, k, terms, ready=None):
                for j in range(k):
                    if ready is not None:
                        pe.wait_ge(op_lo, ready + j + 1)
                    sh, sl, mh, ml = terms(j)
                    pe.matmul(dst, sh, mh, start=j == 0, stop=False)
                    pe.matmul(dst, sh, ml, start=False, stop=False)
                    last = pe.matmul(dst, sl, mh, start=False, stop=j == k - 1)
                return last

            def gemm(slot, width, col, m, k, ops, o0, n, ready=None):
                t = new_tile()
                oh, ol = ops

                def terms(j):
                    a = j * width + col
                    return (Whi[:, slot, a:a + m], Wlo[:, slot, a:a + m],
                            oh[:, o0 + j, 0:n], ol[:, o0 + j, 0:n])

                last = split_product(banks[t.bank][0:m, 0:n], k, terms, ready)
                return t, last

            H, O = (Hhi, Hlo), (Uhi, Ulo)

            def tile_of(m, k, ops, o0, n, ready=None, width=None):
                _, last = gemm(chunk(), width or m, 0, m, k, ops, o0, n, ready)
                last.then_inc(tile_done, 1)

            def total(n):
                pe.wait_ge(sq_summed, at.square.now())
                t = new_tile()
                pe.matmul(banks[t.bank][:, 0:n], ONES[:, :], SUM[:, 0:n], start=True, stop=True).then_inc(tile_done, 1)

            def mod_chunk(q):
                slot = chunk()
                if q == 0 and at.group.n:
                    pe.wait_ge(mod_rows, at.group.now())
                for k in range(DT):
                    for w in (Whi, Wlo):
                        last = pe.matmul(S[0][0:4, q * CW:(q + 1) * CW], CV[:, k, :], w[:, slot, k * CW:(k + 1) * CW],
                                         start=k == 0 and w is Whi, stop=k == DT - 1 and w is Wlo)
                last.then_inc(mod_used, 1)

            def mod_turn():
                if at.group.n:
                    pe.wait_ge(mod_done, at.group.now())
                pe.wait_ge(mod_rows, at.group.next())
                for f in range(GROUP):
                    last = pe.matmul(S[1][:, 2 * f:2 * f + 2], ROW[:, f * P:(f + 1) * P], SEL[:, :],
                                     start=True, stop=True)
                last.then_inc(mod_cols, 1)

            pe.wait_ge(consts, 4)
            pe.wait_ge(shared_in, 48)
            t = new_tile()
            n = CVEC + 2 * DT
            pe.transpose(banks[t.bank][:, 0:n], PST[0:n, 0, 3 * P:4 * P], IDN[0:n, 0:n]).then_inc(tile_done, 1)
            pe.wait_ge(x_in, 32)
            for k in range(DT):
                t = new_tile()
                for j in range(4):
                    src = G[:, 2 * j + k // 4, (k % 4) * P:(k % 4 + 1) * P]
                    last = pe.transpose(banks[t.bank][:, j * P:(j + 1) * P], src, IDN[:, :])
                last.then_inc(tile_done, 1)
                at.square.next()
            pe.wait_ge(vec_in, 16 * N_VEC)
            t = new_tile()
            for b, n in enumerate((ROWS, ROWS, 2 * NMOD * DT)):
                last = pe.transpose(banks[t.bank][:, b * P:b * P + n], PST[0:n, 0, b * P:(b + 1) * P], IDN[0:n, 0:n])
            last.then_inc(tile_done, 1)
            pe.wait_ge(cond_done, 1)
            for q in range(GROUP):
                mod_chunk(q)
            total(T)
            mod_turn()
            with at.loop(pe, 3, chunks=GROUP, groups=1):
                for q in range(GROUP):
                    mod_chunk(q)
                mod_turn()
            for l in range(DEPTH):
                TQ = NS[l] * SEQ
                o = at.operand.n
                seen = [0]

                def projection(m=P, n=TQ):
                    if l == 0:
                        mod_chunk(seen[0] % GROUP)
                    tile_of(m, DT, H, 0, n, o)
                    seen[0] += 1
                    if l == 0 and seen[0] % GROUP == 0:
                        mod_turn()

                projection(n=T)
                projection(n=T)
                at.square.n += 2
                projection(2 * ROPE, T)
                total(T)
                for _ in range(3):
                    projection()
                at.square.n += 3
                for _ in range(2):
                    projection()
                total(TQ)
                for _ in range(8):
                    projection()
                at.operand.n += DT + 5

                units = units_of(l)

                def gate_tile():
                    tile_of(P, DT, H, 0, TQ)

                def pair(first):
                    slot = chunk()
                    wkv = [w[:, slot, 0:4 * P].rearrange("p (k e n) -> p k e n", k=2, e=2) for w in (Whi, Wlo)]
                    pe.wait_ge(op_lo, at.operand.now())
                    keys = new_tile()
                    split_product(banks[keys.bank][:, :], 2,
                                  lambda k: (wkv[0][:, k, 0, :], wkv[1][:, k, 0, :],
                                             Uhi[:, CT0 + k, :], Ulo[:, CT0 + k, :])).then_inc(tile_done, 1)
                    values = new_tile()
                    for tt in range(4):
                        cols = slice(tt * P, (tt + 1) * P)
                        last = split_product(banks[values.bank][:, cols], 2,
                                             lambda k: (Uhi[:, CT0 + k, cols], Ulo[:, CT0 + k, cols],
                                                        wkv[0][:, k, 1, :], wkv[1][:, k, 1, :]))
                    last.then_inc(tile_done, 1)
                    slot = chunk()
                    wq = [w[:, slot, 0:6 * P].rearrange("p (g n) -> p g n", g=6) for w in (Whi, Wlo)]
                    for h in range(2):
                        t = new_tile()
                        split_product(banks[t.bank][:, 0:TQ], 3,
                                      lambda k: (wq[0][:, 2 * k + h, :], wq[1][:, 2 * k + h, :],
                                                 Uhi[:, QT + k, 0:TQ], Ulo[:, QT + k, 0:TQ])).then_inc(tile_done, 1)
                    base = at.unit.n

                    def unit(k):
                        return at.unit.now() - (at.unit.n - base) + k

                    pe.wait_ge(drained[keys.bank], keys.drained)
                    pe.wait_ge(drained[values.bank], values.drained)
                    q0 = at.heads.now()

                    def scores(u):
                        h, col, k0, kt = units[u]
                        pe.wait_ge(q_ready, q0 + h + 1)
                        if u >= 2:
                            pe.wait_ge(exp_done, unit(u - 1))
                        pe.matmul(S[u % 2][:, 0:kt * P], Qb[:, h, col:col + P], Kb[:, h, k0 * P:(k0 + kt) * P],
                                  start=True, stop=True).then_inc(qk_done, 1)

                    def turn(u):
                        kt = units[u][3]
                        pe.wait_ge(prob_done, unit(u + 1))
                        if u:
                            pe.wait_ge(turned_copied, unit(u))
                        for k in range(kt):
                            last = pe.transpose(PT[:, k * P:(k + 1) * P], PR[:, u % 2, k * P:(k + 1) * P], IDN[:, :])
                        last.then_inc(turned, 1)

                    def values_of(u):
                        h, col, k0, kt = units[u]
                        pe.wait_ge(turned_copied, unit(u + 1))
                        for k in range(kt):
                            last = pe.matmul(PV[h * VH:(h + 1) * VH, col:col + P], V[:, k0 + k, h * VH:(h + 1) * VH],
                                             PTs[:, u % 2, k * P:(k + 1) * P], start=k == 0, stop=k == kt - 1)
                        last.then_inc(pv_done, 1)

                    n = len(units)
                    scores(0)
                    scores(1)
                    gate_tile()
                    for u in range(2, n):
                        scores(u)
                        turn(u - 2)
                        if u > 2:
                            values_of(u - 3)
                    turn(n - 2)
                    values_of(n - 3)
                    gate_tile()
                    turn(n - 1)
                    values_of(n - 2)
                    values_of(n - 1)
                    for _ in units:
                        at.unit.next()
                    at.heads.next()
                    at.heads.next()
                    at.operand.next()

                with at.loop(pe, PAIRS - 1, chunks=4, tiles=6, units=len(units), operands=1, heads=2) as i:
                    pair(i)
                pair(None)

                pe.wait_ge(op_lo, at.operand.n)
                def mla():
                    slot = chunk()
                    for q in range(2):
                        _, last = gemm(slot, 2 * CW, q * P, P, 4, O, AT0, TQ)
                        last.then_inc(tile_done, 1)

                def over_channels(src):
                    t = new_tile()
                    for j in range(2):
                        last = pe.matmul(banks[t.bank][:, 0:TQ], ONES[:, :], src[:, j, 0:TQ], start=j == 0, stop=j == 1)
                    last.then_inc(tile_done, 1)

                mla()
                pe.wait_ge(conv_a, l + 1)
                over_channels(ACC)
                mla()
                pe.wait_ge(conv_sq, l + 1)
                over_channels(SQ)
                mla()
                mla()
                at.operand.n += 4

                with at.loop(pe, 4, chunks=12 if l == 0 else 8, tiles=8, groups=1 if l == 0 else 0):
                    for m in range(2):
                        for j in range(2):
                            if l == 0:
                                mod_chunk(2 * m + j)
                            tile_of(P, DT, H, 0, TQ)
                        pe.wait_ge(op_lo, at.operand.n)
                        for o0 in (CO0, SO0):
                            tile_of(P, 2, O, o0, TQ)
                    if l == 0:
                        mod_turn()
                o = at.operand.n
                at.operand.n += DT
                with at.loop(pe, 2, chunks=4, tiles=4):
                    for j in range(4):
                        tile_of(P, DT, H, 0, TQ, o)
                at.square.n += DT
                total(TQ)
                if l == 0:
                    for q in range(GROUP):
                        mod_chunk(q)
                    mod_turn()
                o = at.operand.n
                at.operand.n += DT
                for g, n in enumerate(FF_GROUPS):
                    mixed = 1 if l == 0 else 0
                    with at.loop(pe, n // 2, chunks=4 + 4 * mixed, tiles=4, operands=2, groups=mixed):
                        for j in range(4):
                            if mixed:
                                mod_chunk(j)
                            tile_of(P, DT, H, 0, TQ, o)
                        at.operand.next()
                        at.operand.next()
                        if mixed:
                            mod_turn()
                    up = at.operand.n - n
                    if g == len(FF_GROUPS) - 1 and l == DEPTH - 1:
                        for j in range(8):
                            tile_of(P, n, O, 0, TQ, up)
                    else:
                        with at.loop(pe, 2, chunks=4, tiles=4):
                            for j in range(4):
                                tile_of(P, n, O, 0, TQ, up)
                at.square.n += DT
                total(SEQ if l == DEPTH - 1 else T)
            pe.wait_ge(fin_z, DT)
            for j in range(2):
                for h in range(2):
                    t = new_tile()
                    for k in range(4):
                        last = pe.transpose(banks[t.bank][:, k * P:(k + 1) * P],
                                            G[:, 4 * h + k, j * P:(j + 1) * P], IDN[:, :])
                    last.then_inc(tile_done, 1)


_INS = ["x", "c", "ctx", "c_ctx", "w_mod", "b_mod", "ln1_g", "w_in", "q_a_norm_g", "w_q_b", "kv_a_norm_g",
        "w_kv_b", "w_mla_o", "conv_dw", "conv_dw_b", "conv_ln_g", "conv_ln_b", "w_conv_o", "sc_dw", "w_sc_o",
        "w_o", "ln2_g", "w_ff1", "w_ff3", "w_ff2", "final_g"]


def kernel(**inputs):
    import numpy as np
    import concourse.bacc as bacc
    from concourse.bass_utils import run_bass_kernel_spmd

    nc = bacc.Bacc("TRN2", target_bir_lowering=False, num_devices=1)
    arrays, args = {}, []
    for name in _INS:
        a = np.ascontiguousarray(inputs[name])
        arrays[f"in_{name}"] = a
        args.append(nc.dram_tensor(f"in_{name}", a.shape, mybir.dt.from_np(a.dtype), kind="ExternalInput").ap())
    token = np.arange(SEQ)
    inv = np.power(np.float32(10000.0), -np.arange(0, ROPE // 2, 2, dtype=np.float32) / np.float32(ROPE // 2))
    cos, sin = np.ones((ROPE, T), np.float32), np.zeros((ROPE, T), np.float32)
    for r in range(ROPE):
        pos = (token // GRID_W if r < ROPE // 2 else token % GRID_W).astype(np.float32)
        angle = pos * inv[r % 8]
        cos[r, :SEQ] = np.cos(angle)
        sin[r, :SEQ] = np.sin(angle) * (-1 if r % 16 < 8 else 1)
    arrays["rope"] = np.concatenate([cos, sin, cos, sin])
    args.append(nc.dram_tensor("rope", (P, T), mybir.dt.float32, kind="ExternalInput").ap())
    args.append(nc.dram_tensor("out", (1, SEQ, D), mybir.dt.float32, kind="ExternalOutput").ap())
    build(nc, *args)
    r = run_bass_kernel_spmd(nc, [arrays], core_ids=[0])
    return r.results[0]["out"]
```

```python
from contextlib import ExitStack, contextmanager

import concourse.bass as bass
from concourse import mybir

D = 1024
SEQ = 256
DEPTH = 2
HEADS, NOPE, ROPE, VH = 8, 64, 32, 64
QL, KVL = 384, 256
CH = 256
TAPS, SC_TAPS = 31, 3
GRID_W = 64
EPS = 1e-6
P = 128
DT = D // P
T = 2 * SEQ
KV0 = QL
ROPE0 = KV0 + KVL
GLU0 = ROPE0 + ROPE
SC0 = GLU0 + 2 * CH
GATE0 = SC0 + 3 * CH
SCALE = (NOPE + ROPE) ** -0.5
CW = P
SLOTS = 4
SLOT = DT * CW
NMOD = 6
GROUP = 4

LN1, LN2, QG, KVG, CB, LNG, LNB, CDW, SCW = 0, 8, 16, 19, 21, 23, 25, 27, 27 + 2 * TAPS
ROWS = SCW + 2 * SC_TAPS
N_VEC = 9 + 1 + 1
FING, CVEC = 0, 8
TAPS_BEFORE, TAPS_PER_PAIR = 3, 7
PAIRS = HEADS // 2
FF_GROUPS = [8, 8, 6]


PAIR_KINDS = ["keys", "queries", "plain", "plain"]


AHEAD = 3


def with_mods(kinds, l):
    res, j = [], 0
    for k in kinds:
        if l or k == "short":
            res.append(k)
        else:
            res += [k, "plain"] if j % GROUP < GROUP - 1 else ["plain", k]
            j += 1
    return res


def projection_kinds(l):
    return with_mods(["plain"] * AHEAD + ["rope"] + ["plain"] * 12, l)


def branch_kinds(l):
    return with_mods(["plain", "plain", "short", "short"] * 2, l)


def ahead(kinds, after):
    return iter((kinds + after[:AHEAD])[AHEAD:])


class Tally:

    def __init__(self):
        self.n, self.var, self.step = 0, None, 0

    def now(self):
        return self.n if self.var is None else self.var * self.step + self.n

    def next(self):
        self.n += 1
        return self.now()


@contextmanager
def turns(eng, times, steps):
    before = [(t, t.n, k) for t, k in steps]
    with eng.Fori(0, times) as i:
        for t, _, k in before:
            t.var, t.step = i, k
        yield i
    for t, n, k in before:
        assert t.n - n == k, (t.n - n, k, steps.index((t, k)))
        t.n, t.var, t.step = n + k * times, None, 0


class Tile:

    def __init__(self, bank, done, before, drained):
        self.bank, self.done, self.before, self.drained = bank, done, before, drained


class Place:

    def __init__(self):
        self.chunk, self.tiles, self.operand, self.unit, self.square, self.heads, self.gates, self.group = (Tally() for _ in range(8))
        self.uses = [Tally() for _ in range(4)]
        self.ring = 0
        self.z = 0
        self.split_by_slot = False

    def tile(self):
        b = self.ring % 4
        self.ring += 1
        before = self.uses[b].now()
        return Tile(b, self.tiles.next(), before, self.uses[b].next())

    @contextmanager
    def loop(self, eng, times, chunks=0, tiles=0, operands=0, units=0, squares=0, heads=0, gates=0, groups=0, extra=()):
        self.ring = 0
        steps = [(self.chunk, chunks), (self.tiles, tiles), (self.operand, operands),
                 (self.unit, units), (self.square, squares), (self.heads, heads), (self.gates, gates), (self.group, groups), *extra]
        steps += [(u, (tiles - b + 3) // 4 if tiles > b else 0) for b, u in enumerate(self.uses)]
        assert times > 1 and chunks % SLOTS == 0
        with turns(eng, times, steps) as i:
            yield i
        self.ring = 0


def build(nc, x, c, ctx_in, c_ctx, w_mod, b_mod, ln1_g, w_in, q_a_norm_g, w_q_b, kv_a_norm_g,
          w_kv_b, w_mla_o, conv_dw, conv_dw_b, conv_ln_g, conv_ln_b, w_conv_o, sc_dw, w_sc_o,
          w_o, ln2_g, w_ff1, w_ff3, w_ff2, final_g, rope, out):
    F32, F32R = mybir.dt.float32, mybir.dt.float32r
    ACT, ALU, AX = mybir.ActivationFunctionType, mybir.AluOpType, mybir.AxisListType

    stack = ExitStack()
    with stack:
        def sb(name, shape, dt=F32):
            return stack.enter_context(nc.sbuf_tensor(name, shape, dt))

        def sem(name):
            return stack.enter_context(nc.semaphore(name))

        X = sb("X", [P, DT, T])
        Wraw = sb("Wraw", [P, SLOTS, SLOT])
        Whi = sb("Whi", [P, SLOTS, SLOT], F32R)
        Wlo = sb("Wlo", [P, SLOTS, SLOT], F32R)
        Hhi = sb("Hhi", [P, DT, T], F32R)
        Hlo = sb("Hlo", [P, DT, T], F32R)
        G = sb("G", [P, DT, T])
        Uhi = sb("Uhi", [P, 9, T], F32R)
        Ulo = sb("Ulo", [P, 9, T], F32R)
        QT, CT0, AT0, CO0, SO0 = 0, 3, 5, 0, 2
        Qb = sb("Qb", [96, 2, T])
        Kb = sb("Kb", [96, 2, T])
        V = sb("V", [P, 4, P])
        PR = sb("PR", [P, 2, T])
        PTs = sb("PTs", [P, 2, T])
        PAD = TAPS // 2
        U = sb("U", [P, 2, 2, SEQ + 2 * PAD])
        ACC = sb("ACC", [P, 2, T])
        C = sb("C", [P, 2, 2, SEQ + 2])
        BG = sb("BG", [P, 2, T])
        SQ = sb("SQ", [P, 2, T])
        SUM = sb("SUM", [P, T])
        ROOT = sb("ROOT", [P, T])
        RSTD = sb("RSTD", [P, T])
        Z = sb("Z", [P, 2, T])
        TG = sb("TG", [P, 2, T])
        TAB = sb("TAB", [P, T])
        IDN = sb("IDN", [P, P])
        ONES = sb("ONES", [P, P])
        PAR = sb("PAR", [P, 4, P])
        MOD = sb("MOD", [P, DEPTH, NMOD * DT, 2])
        AV = sb("AV", [P, DT, 2])
        CTH = sb("CTH", [P, 16])
        CS = sb("CS", [P, 2, DT])
        CV = sb("CV", [P, DT, 4], F32R)
        SEL = sb("SEL", [4, 2])
        ROW = PTs[0:4, 0, :]
        WARM = sb("WARM", [P, 8])
        NM = sb("NM", [P, 2])
        RS = sb("RS", [P, 2])
        RR = sb("RR", [P, 2])
        PST = TG

        banks = [stack.enter_context(nc.psum_tensor(f"bank{b}", [P, T], F32)) for b in range(4)]
        S = [stack.enter_context(nc.psum_tensor(f"scores{b}", [P, T], F32)) for b in range(2)]
        PT = stack.enter_context(nc.psum_tensor("probsT", [P, T], F32))
        PV = stack.enter_context(nc.psum_tensor("attended", [P, T], F32))

        x_in = sem("x_in")
        shared_in = sem("shared_in")
        vec_in = sem("vec_in")
        consts = sem("consts")
        padded = sem("padded")
        raw_in = [sem(f"raw_in{b}") for b in range(SLOTS)]
        slot_free = sem("slot_free")
        hi_done = sem("hi_done")
        lo_done = [sem(f"lo_done{b}") for b in range(SLOTS)]
        mod_used = sem("mod_used")
        mod_rows = sem("mod_rows")
        mod_cols = sem("mod_cols")
        mod_done = sem("mod_done")
        tile_done = sem("tile_done")
        drained = [sem(f"drained{b}") for b in range(4)]
        sq_done = sem("sq_done")
        sq_summed = sem("sq_summed")
        root_done = sem("root_done")
        z_done = sem("z_done")
        op_hi = sem("op_hi")
        op_lo = sem("op_lo")
        q_nope = sem("q_nope")
        qk_done = sem("qk_done")
        max_done = sem("max_done")
        exp_done = sem("exp_done")
        prob_done = sem("prob_done")
        turned = sem("turned")
        turned_copied = sem("turned_copied")
        pv_done = sem("pv_done")
        dve_step = sem("dve_step")
        gate_tanh = sem("gate_tanh")
        out_ready = sem("out_ready")
        pool_step = sem("pool_step")
        conv_sq = sem("conv_sq")
        conv_v = sem("conv_v")
        conv_t = sem("conv_t")
        conv_s = sem("conv_s")
        q_ready = sem("q_ready")
        cond_tanh = sem("cond_tanh")
        cond_done = sem("cond_done")
        conv_a = sem("conv_a")
        fin_z = sem("fin_z")
        stored = sem("stored")

        block = stack.enter_context(nc.Block())

        def parts(kind, slot):
            if kind in ("plain", "short"):
                n = SLOT if kind == "plain" else SLOT // 4
                return [(Wraw[:, slot, 0:n], Whi[:, slot, 0:n], Wlo[:, slot, 0:n])]
            if kind == "keys":
                raw = Wraw[:, slot, 0:4 * P].rearrange("p (k h e d) -> p k h e d", k=2, h=2, e=2)
                both = [w[:, slot, 0:4 * P].rearrange("p (k e h d) -> p k e h d", k=2, h=2, e=2) for w in (Whi, Wlo)]
                return [(raw[:, :, :, e, :], both[0][:, :, e, :, :], both[1][:, :, e, :, :]) for e in range(2)]
            if kind == "rope":
                groups, raw_w, packed_w, at = DT, ROPE, 2 * ROPE, 0
            else:
                groups, raw_w, packed_w, at = 6, NOPE + ROPE, P, NOPE
            src = Wraw[:, slot, 0:groups * raw_w].rearrange("p (g n) -> p g n", g=groups)
            dst = [w[:, slot, 0:groups * packed_w].rearrange("p (g n) -> p g n", g=groups) for w in (Whi, Wlo)]
            res = [(src, dst[0][:, :, 0:raw_w], dst[1][:, :, 0:raw_w])]
            for g in range(2):
                for b in range(2):
                    s0, d0 = at + 16 * g + 8 * (1 - b), raw_w + 16 * g + 8 * b
                    res.append((src[:, :, s0:s0 + 8], dst[0][:, :, d0:d0 + 8], dst[1][:, :, d0:d0 + 8]))
            return res

        def split_hi(act, at, kind, mods=0):
            slot, n = at.chunk.n % SLOTS, at.chunk.n
            if at.chunk.var is None:
                act.wait_ge(raw_in[slot], 16 * (n // SLOTS + 1))
            else:
                act.wait_ge(raw_in[slot], at.chunk.var * (16 * at.chunk.step // SLOTS) + 16 * (n // SLOTS + 1))
            if at.tiles.n:
                act.wait_ge(tile_done, at.tiles.now())
            if mods:
                act.wait_ge(mod_used, at.group.now() * GROUP + mods)
            for raw, hi, _ in parts(kind, slot):
                last = act.activation(hi, raw, ACT.Copy)
            last.then_inc(hi_done, 1)
            at.chunk.next()

        def split_lo(eng, mine, at, kind):
            slot = at.chunk.n % SLOTS
            if slot % 2 == mine if at.split_by_slot else mine:
                eng.wait_ge(hi_done, at.chunk.now() + 1)
                for raw, hi, lo in parts(kind, slot):
                    last = eng.tensor_tensor(lo, raw, hi.bitcast(F32), ALU.subtract)
                last.then_inc(lo_done[slot], 1)
            at.chunk.next()

        NS = [2, 1]
        half = [slice(s * SEQ, (s + 1) * SEQ) for s in range(2)]

        def by_stream(ap, l):
            return ap.rearrange("p (s n) -> p s n", s=2)[:, 0:NS[l], :]

        def units_of(l):
            return [(h, s * SEQ + q * P, 2 * s, 4 - 2 * s)
                    for h in range(2) for s in range(NS[l]) for q in range(2)]

        def stat_root(l, k):
            return 5 * l + k + 1

        @block.sync
        def _(sp):
            at = Place()
            for row, v in ((CVEC, c[0]), (CVEC + DT, c_ctx), (FING, final_g)):
                sp.dma_start(PST[row:row + DT, 0, 3 * P:4 * P],
                             v.rearrange("(t p) -> t p", p=P)).then_inc(shared_in, 16)

            def load(w, row0, k, col, width):
                slot, n = at.chunk.n % SLOTS, at.chunk.n
                if at.chunk.var is not None:
                    sp.wait_ge(lo_done[slot], at.chunk.var * (at.chunk.step // SLOTS) + n // SLOTS)
                    sp.sem_inc(slot_free, 1)
                elif n >= SLOTS:
                    sp.wait_ge(lo_done[slot], n // SLOTS)
                sp.dma_start(Wraw[:, slot, 0:k * width].rearrange("p (k n) -> p k n", k=k),
                             w[row0:row0 + k * P, bass.ds(col, width)].rearrange(
                                 "(k p) n -> p k n", p=P)).then_inc(raw_in[slot], 16)
                at.chunk.next()

            def mod(l, n):
                load(w_mod[l], 0, DT, n * CW, CW)

            for n in range(GROUP - 1):
                mod(0, n)
            sp.dma_start(G[:, 0:4, :].rearrange("p (t h) n -> p t (h n)", t=2),
                         x[0].rearrange("(t p) d -> p t d", p=P)).then_inc(x_in, 16)
            mod(0, GROUP - 1)
            sp.dma_start(G[:, 4:8, :].rearrange("p (t h) n -> p t (h n)", t=2),
                         ctx_in[0].rearrange("(t p) d -> p t d", p=P)).then_inc(x_in, 16)
            sp.dma_start(PST[0:2 * NMOD * DT, 0, 2 * P:3 * P],
                          b_mod.rearrange("l (t p) -> (l t) p", p=P)).then_inc(vec_in, 16)
            for row, v in ((LN1, ln1_g), (LN2, ln2_g), (QG, q_a_norm_g), (KVG, kv_a_norm_g),
                           (CB, conv_dw_b), (LNG, conv_ln_g), (LNB, conv_ln_b)):
                n = v.shape[1] // P
                sp.dma_start(PST[row:row + n, 0, 0:2 * P].rearrange("t (l p) -> t l p", l=2),
                              v.rearrange("l (t p) -> t l p", p=P)).then_inc(vec_in, 16)
            for row, v in ((CDW, conv_dw), (SCW, sc_dw)):
                n = v.shape[1] * v.shape[2] // P
                sp.dma_start(PST[row:row + n, 0, 0:2 * P].rearrange("t (l p) -> t l p", l=2),
                              v.rearrange("l w (t p) -> (w t) l p", p=P)).then_inc(vec_in, 16)
            sp.dma_start(TAB[:, :], rope).then_inc(vec_in, 16)
            for n in range(GROUP, 4 * GROUP):
                mod(0, n)

            def mixed(j, chunk, mod_chunk):
                for go in ((chunk, mod_chunk) if j % GROUP < GROUP - 1 else (mod_chunk, chunk)):
                    go()
            for l in range(DEPTH):
                wi = w_in[l]
                cols = [KV0, KV0 + CW, GLU0 + CH, ROPE0, 0, CW, 2 * CW, GLU0 + CH + CW]
                cols += [c0 + j * CW for c0 in (GLU0, SC0 + CH, SC0 + 2 * CH, SC0) for j in range(2)]
                for n, col in enumerate(cols):
                    def go():
                        load(wi, 0, DT, col, ROPE if col == ROPE0 else CW)
                    if l == 0:
                        mixed(n, go, lambda: mod(0, 16 + n))
                    else:
                        go()

                def pair(p):
                    n = 2 * (NOPE + ROPE)
                    load(w_kv_b[l], 0, 2, p * (2 * P), 2 * P)
                    load(w_q_b[l], 0, 3, p * n, n)
                    for j in range(2):
                        load(wi, 0, DT, p * (2 * CW) + (GATE0 + j * CW), CW)

                with at.loop(sp, PAIRS - 1, chunks=4) as i:
                    pair(i)
                pair(PAIRS - 1)
                for j in range(4):
                    load(w_mla_o[l], 0, 4, j * 2 * CW, 2 * CW)
                with at.loop(sp, 4, chunks=12 if l == 0 else 8) as i:
                    for j in range(2):
                        for b in range(2):
                            def go():
                                load(wi, 0, DT, i * (2 * CW) + (GATE0 + (b + 1) * D + j * CW), CW)
                            if l == 0:
                                mixed(2 * j + b, go, lambda: load(
                                    w_mod[0], 0, DT, i * (4 * CW) + (32 + 2 * j + b) * CW, CW))
                            else:
                                go()
                        for w in (w_conv_o, w_sc_o):
                            load(w[l], 0, 2, i * (2 * CW) + j * CW, CW)
                for j in range(DT):
                    def go():
                        load(w_o[l], 0, DT, j * CW, CW)
                    if l == 0 and j >= GROUP:
                        mixed(j, go, lambda: mod(1, j - GROUP))
                    else:
                        go()
                g0 = 0
                for n in FF_GROUPS:
                    with at.loop(sp, n // 2, chunks=8 if l == 0 else 4) as i:
                        for b, w in enumerate((w_ff1, w_ff3)):
                            for j in range(2):
                                def go():
                                    load(w[l], 0, DT, i * (2 * CW) + (g0 + j) * P, CW)
                                if l == 0:
                                    mixed(2 * b + j, go, lambda: load(
                                        w_mod[1], 0, DT, i * (GROUP * CW) + (GROUP + 2 * g0 + 2 * b + j) * CW, CW))
                                else:
                                    go()
                    with at.loop(sp, 2, chunks=4) as i:
                        for j in range(4):
                            load(w_ff2[l], g0 * P, n, i * (4 * CW) + j * CW, CW)
                    g0 += n
            for h in range(2):
                for j in range(2):
                    sp.wait_ge(out_ready, 2 * h + j + 1)
                    sp.dma_start(out[0, j * P:(j + 1) * P, h * T:(h + 1) * T],
                                 X[:, 2 * h + j, :]).then_inc(stored, 16)
            sp.wait_ge(stored, 64)

        @block.gpsimd
        def _(pool):
            at = Place()
            step = Tally()

            def mark(ins):
                ins.then_inc(pool_step, 1)
                return step.next()

            mark(pool.memset(IDN[:, :], 0.0))
            v = mark(pool.memset(SEL[:, :], 0.0))
            pool.memset(ONES[:, :], 1.0).then_inc(consts, 1)
            pool.wait_ge(pool_step, v)
            pool.affine_select(out=IDN[:, :], in_=IDN[:, :], compare_op=ALU.not_equal, fill=1.0,
                               base=0, pattern=[[-1, P]], channel_multiplier=1).then_inc(consts, 1)
            v = mark(pool.affine_select(out=SEL[:, :], in_=SEL[:, :], compare_op=ALU.not_equal, fill=1.0,
                                        base=0, pattern=[[-1, 2]], channel_multiplier=1))
            pool.wait_ge(pool_step, v)
            pool.affine_select(out=SEL[:, :], in_=SEL[:, :], compare_op=ALU.not_equal, fill=1.0,
                               base=-2, pattern=[[-1, 2]], channel_multiplier=1).then_inc(consts, 1)
            pool.memset(U[:, :, :, :].rearrange("p a b c -> p (a b c)"), 0.0).then_inc(padded, 1)
            pool.memset(C[:, :, :, :].rearrange("p a b c -> p (a b c)"), 0.0).then_inc(padded, 1)

            def clear_sum(roots):
                if roots:
                    pool.wait_ge(root_done, roots)
                v = mark(pool.memset(SUM[:, :], 0.0))
                pool.wait_ge(pool_step, v)

            def add_square(n):
                slot = at.square.n % 2
                if at.square.n:
                    pool.wait_ge(sq_summed, at.square.now())
                pool.wait_ge(sq_done, at.square.now() + 1)
                pool.tensor_tensor(SUM[:, 0:n], SUM[:, 0:n], SQ[:, slot, 0:n], ALU.add).then_inc(sq_summed, 1)
                at.square.next()

            def look(kind="plain"):
                split_lo(pool, 0, at, kind)

            clear_sum(0)
            for _ in range(AHEAD + 4 * GROUP):
                look()
            at.split_by_slot = True
            for _ in range(DT):
                add_square(T)
            for l in range(DEPTH):
                TQ = NS[l] * SEQ
                nxt = ahead(projection_kinds(l), PAIR_KINDS)

                def step_in():
                    for _ in range(2 if l == 0 else 1):
                        look(next(nxt))

                clear_sum(stat_root(l, 0))
                for _ in range(2):
                    step_in()
                    add_square(T)
                step_in()
                step_in()
                clear_sum(stat_root(l, 1))
                for _ in range(3):
                    step_in()
                    add_square(TQ)
                for _ in range(9):
                    step_in()
                with at.loop(pool, PAIRS - 1, chunks=4):
                    for kind in ahead(PAIR_KINDS, PAIR_KINDS):
                        look(kind)
                for kind in ahead(PAIR_KINDS + ["plain"] * 4, branch_kinds(l)):
                    look(kind)
                with at.loop(pool, 3, chunks=12 if l == 0 else 8):
                    for kind in ahead(branch_kinds(l), branch_kinds(l)):
                        look(kind)
                for kind in ahead(branch_kinds(l), ["plain"] * AHEAD):
                    look(kind)
                clear_sum(stat_root(l, 2))
                for j in range(DT):
                    for _ in range(2 if l == 0 and j >= GROUP else 1):
                        look()
                    add_square(TQ)
                for g, n in enumerate(FF_GROUPS):
                    last = g == len(FF_GROUPS) - 1
                    with at.loop(pool, n // 2, chunks=8 if l == 0 else 4):
                        for _ in range(8 if l == 0 else 4):
                            look()
                    if last:
                        clear_sum(stat_root(l, 4))
                    if last and l == DEPTH - 1:
                        for j in range(8):
                            if j < DT - AHEAD:
                                look()
                            add_square(TQ)
                    else:
                        with at.loop(pool, 2, chunks=4, squares=4 * last):
                            for _ in range(4):
                                look()
                                if last:
                                    add_square(TQ)

        @block.scalar
        def _(act):
            at = Place()

            def look(kind="plain", mods=0):
                split_hi(act, at, kind, mods)

            def enter(j, mixed, nxt=None):
                kind = next(nxt) if nxt else "plain"
                look(kind, mods=j % GROUP if mixed else 0)
                if mixed and j % GROUP == GROUP - 1:
                    look(next(nxt) if nxt else "plain", mods=GROUP)
                    mod_row()

            def leave(j, mixed, nxt=None):
                if mixed and j % GROUP < GROUP - 1:
                    look(next(nxt) if nxt else "plain")

            def copy_out(dst, n=T, func=ACT.Copy, scale=1.0, m=P):
                t = at.tile()
                act.wait_ge(tile_done, t.done)
                act.activation(dst, banks[t.bank][0:m, 0:n], func, scale=scale).then_inc(drained[t.bank], 1)
                return t

            def square(src, n):
                slot = at.square.n % 2
                if at.square.n >= 2:
                    act.wait_ge(sq_summed, at.square.now() - 1)
                act.activation(SQ[:, slot, 0:n], src, ACT.Square).then_inc(sq_done, 1)
                at.square.next()

            def root(n, width):
                t = at.tile()
                act.wait_ge(tile_done, t.done)
                act.activation(ROOT[:, 0:n], banks[t.bank][:, 0:n], ACT.Sqrt, bias=EPS,
                               scale=1.0 / width).then_inc(root_done, 1)

            warmed = iter(range(8))

            def load_sqrt():
                w = next(warmed)
                act.activation(WARM[:, w:w + 1], ONES[:, 0:1], ACT.Sqrt)

            def mod_row(bank=0):
                group = at.group.now()
                act.wait_ge(mod_used, group * GROUP + GROUP)
                if at.group.n:
                    act.wait_ge(mod_cols, group)
                act.activation(ROW, S[bank][0:4, :], ACT.Copy).then_inc(mod_rows, 1)
                at.group.next()

            def operand(dst, src, z=True, scale=1.0):
                if z:
                    at.z += 1
                    act.wait_ge(z_done, at.z)
                act.activation(dst, src, ACT.Copy, scale=scale).then_inc(op_hi, 1)
                at.operand.next()

            def normed_h(l, mod, n_streams):
                for k in range(DT):
                    at.z += 1
                    act.wait_ge(z_done, at.z)
                    for s in range(n_streams):
                        last = act.activation(Hhi[:, k, half[s]], Z[:, k % 2, half[s]], ACT.Identity,
                                              bias=MOD[:, l, mod * DT + k, s:s + 1])
                    last.then_inc(op_hi, 1)
                    at.operand.next()

            act.wait_ge(consts, 1)
            t = at.tile()
            act.wait_ge(drained[t.bank], t.drained)
            act.activation(CTH[:, :], PAR[:, 3, CVEC:CVEC + 2 * DT], ACT.Tanh, scale=0.5).then_inc(cond_tanh, 1)
            for _ in range(AHEAD):
                look()
            for g in range(4):
                for q in range(GROUP):
                    if q == 0 and g:
                        look(mods=GROUP)
                        mod_row((g - 1) % 2)
                    else:
                        look(mods=q)
                    if g == 0 and q == 0:
                        load_sqrt()
                    if g in (1, 2):
                        k = (g - 1) * GROUP + q
                        t = at.tile()
                        act.wait_ge(drained[t.bank], t.drained)
                        square(X[:, k, :], T)
                if g == 0:
                    at.tile()
            root(T, D)
            mod_row(1)
            for l in range(DEPTH):
                TQ = NS[l] * SEQ
                normed_h(l, 0, 2)
                nxt = ahead(projection_kinds(l), PAIR_KINDS)
                tile_no = 0

                def step_in():
                    enter(tile_no, l == 0, nxt)

                def step_out():
                    nonlocal tile_no
                    leave(tile_no, l == 0, nxt)
                    tile_no += 1

                for j in range(2):
                    step_in()
                    t = at.tile()
                    act.wait_ge(tile_done, t.done)
                    square(banks[t.bank][:, :], T)
                    step_out()
                step_in()
                copy_out(TG[:, 0, 0:TQ], TQ, ACT.Tanh, 0.5)
                step_out()
                step_in()
                at.tile()
                step_out()
                step_in()
                root(T, KVL)
                for k in range(2):
                    operand(Uhi[:, CT0 + k, :], Z[:, k % 2, :])
                for j in range(3):
                    if j:
                        step_in()
                    t = at.tile()
                    act.wait_ge(tile_done, t.done)
                    square(banks[t.bank][:, 0:TQ], TQ)
                    step_out()
                step_in()
                copy_out(TG[:, 1, 0:TQ], TQ, ACT.Tanh, 0.5)
                step_out()
                root(TQ, QL)
                for k in range(3):
                    operand(Uhi[:, QT + k, 0:TQ], Z[:, k % 2, 0:TQ])
                glu = []
                for j in range(2):
                    step_in()
                    glu.append(at.tile())
                    step_out()
                for j in range(2):
                    step_in()
                    act.wait_ge(drained[glu[j].bank], glu[j].drained)
                    copy_out(TG[:, j, 0:TQ], TQ)
                    step_out()
                for j in range(2):
                    step_in()
                    at.tile()
                    step_out()
                for j in range(2):
                    step_in()
                    copy_out(BG[:, j, 0:TQ], TQ)
                    step_out()

                units = units_of(l)

                def pair(p, after):
                    nxt = ahead(PAIR_KINDS, after)
                    look(next(nxt))
                    t = at.tile()
                    act.wait_ge(tile_done, t.done)
                    for h in range(2):
                        last = act.activation(Kb[0:NOPE, h, :], banks[t.bank][h * NOPE:(h + 1) * NOPE, :], ACT.Copy)
                    last.then_inc(drained[t.bank], 1)
                    copy_out(V[:, :, :].rearrange("p t n -> p (t n)"))
                    look(next(nxt))
                    for h in range(2):
                        t = at.tile()
                        act.wait_ge(tile_done, t.done)
                        act.activation(Qb[0:NOPE, h, 0:TQ], banks[t.bank][0:NOPE, 0:TQ], ACT.Copy,
                                       scale=SCALE).then_inc(q_nope, 1)

                    base = at.unit.n

                    def unit(k):
                        return at.unit.now() - (at.unit.n - base) + k

                    def exps(u):
                        kt = units[u][3]
                        act.wait_ge(max_done, unit(u + 1))
                        if u >= 2:
                            act.wait_ge(turned, unit(u - 1))
                        act.activation(PR[:, u % 2, 0:kt * P], S[u % 2][:, 0:kt * P], ACT.Exp,
                                       bias=NM[:, u % 2:u % 2 + 1],
                                       accum_out=RS[:, u % 2:u % 2 + 1]).then_inc(exp_done, 1)
                        at.unit.next()

                    def copy_turned(u):
                        kt = units[u][3]
                        act.wait_ge(turned, unit(u + 1))
                        if u >= 2:
                            act.wait_ge(pv_done, unit(u - 1))
                        act.activation(PTs[:, u % 2, 0:kt * P], PT[:, 0:kt * P], ACT.Copy).then_inc(turned_copied, 1)

                    exps(0)
                    exps(1)
                    look(next(nxt))
                    for u in range(2, len(units)):
                        copy_turned(u - 2)
                        exps(u)
                    copy_turned(len(units) - 2)
                    copy_out(G[:, p * 2, 0:TQ], TQ, ACT.Tanh, 0.5)
                    copy_turned(len(units) - 1)
                    look(next(nxt))
                    copy_out(G[:, p * 2 + 1, 0:TQ], TQ, ACT.Tanh, 0.5)
                    act.wait_ge(pv_done, at.unit.now())
                    act.activation(Uhi[:, p + AT0, 0:TQ], PV[:, 0:TQ], ACT.Copy).then_inc(op_hi, 1)
                    at.operand.next()

                with at.loop(act, PAIRS - 1, chunks=4, tiles=6, units=len(units), operands=1) as i:
                    pair(i, PAIR_KINDS)
                pair(PAIRS - 1, ["plain"] * AHEAD)

                nxt = ahead(["plain"] * 4, branch_kinds(l))
                look(next(nxt))
                act.wait_ge(conv_a, l + 1)
                for j in range(2):
                    operand(Uhi[:, SO0 + j, 0:TQ], BG[:, j, 0:TQ], z=False)
                at.tile()
                at.tile()
                look(next(nxt))
                mean = at.tile()
                act.wait_ge(drained[mean.bank], mean.drained)
                for j in range(2):
                    last = act.activation(SQ[:, j, 0:TQ], ACC[:, j, 0:TQ], ACT.Square)
                last.then_inc(conv_sq, 1)
                at.tile()
                at.tile()
                look(next(nxt))
                root(TQ, CH)
                act.wait_ge(conv_v, l + 1)
                for j in range(2):
                    last = act.activation(TG[:, j, 0:TQ], ACC[:, j, 0:TQ], ACT.Tanh, scale=0.5)
                last.then_inc(conv_t, 1)
                act.wait_ge(conv_s, l + 1)
                for j in range(2):
                    operand(Uhi[:, CO0 + j, 0:TQ], Z[:, j, 0:TQ], z=False, scale=0.5)
                for _ in range(2):
                    at.tile()
                look(next(nxt))
                for _ in range(2):
                    at.tile()

                def branches(after):
                    nxt = ahead(branch_kinds(l), after)
                    free = [(2 + j, at.uses[2 + j].now()) for j in range(2)]
                    for m in range(2):
                        for j in range(2):
                            enter(2 * m + j, l == 0, nxt)
                            act.wait_ge(drained[free[j][0]], free[j][1])
                            copy_out(TG[:, j, 0:TQ], TQ, ACT.Tanh, 0.5)
                            leave(2 * m + j, l == 0, nxt)
                        free = []
                        for j in range(2):
                            look(next(nxt), mods=2 if l == 0 and m == 0 and j == 0 else 0)
                            t = at.tile()
                            free.append((t.bank, t.drained))

                with at.loop(act, 3, chunks=12 if l == 0 else 8, tiles=8, groups=1 if l == 0 else 0):
                    branches(branch_kinds(l))
                at.ring = 0
                branches(["plain"] * AHEAD)
                summed = [u.now() for u in at.uses]
                act.wait_ge(tile_done, at.tiles.now() - 2)
                for k in range(DT):
                    if k == 0 or k == DT - 1:
                        act.wait_ge(drained[3], summed[3] - (1 if k == 0 else 0))
                    operand(Hhi[:, k, 0:TQ], G[:, k, 0:TQ], z=False, scale=0.5)

                def residual_squares(m):
                    t = at.tile()
                    act.wait_ge(drained[t.bank], t.drained)
                    square(X[:, m, 0:TQ], TQ)

                load_sqrt()
                for j in range(DT):
                    mixed = l == 0 and j >= GROUP
                    enter(j, mixed)
                    residual_squares(j)
                    leave(j, mixed)
                root(TQ, D)
                normed_h(l, 3, NS[l])
                for g, n in enumerate(FF_GROUPS):
                    last = g == len(FF_GROUPS) - 1
                    mixed = 1 if l == 0 else 0
                    with at.loop(act, n // 2, chunks=4 + 4 * mixed, tiles=4, operands=2, groups=mixed) as i:
                        for j in range(2):
                            enter(j, mixed)
                            t = at.tile()
                            act.wait_ge(tile_done, t.done)
                            act.activation(TG[:, j, 0:TQ], banks[t.bank][:, 0:TQ], ACT.Tanh,
                                           scale=0.5).then_inc(gate_tanh, 1)
                            leave(j, mixed)
                        for j in range(2):
                            enter(2 + j, mixed)
                            t = at.tile()
                            act.wait_ge(drained[t.bank], t.drained)
                            act.activation(Uhi[:, i * 2 + j, 0:TQ], PR[:, j, 0:TQ],
                                           ACT.Copy).then_inc(op_hi, 1)
                            at.operand.next()
                            leave(2 + j, mixed)
                    if last:
                        load_sqrt()
                    if last and l == DEPTH - 1:
                        for j in range(8):
                            if j < DT - AHEAD:
                                look()
                            residual_squares(j)
                    else:
                        with at.loop(act, 2, chunks=4, tiles=4, squares=4 * last) as i:
                            for j in range(4):
                                look()
                                if last:
                                    residual_squares(i * 4 + j)
                                else:
                                    at.tile()
                root(SEQ if l == DEPTH - 1 else T, D)
            act.wait_ge(fin_z, DT)
            for h in range(2):
                for j in range(2):
                    t = at.tile()
                    act.wait_ge(tile_done, t.done)
                    act.activation(X[:, 2 * h + j, :], banks[t.bank][:, :], ACT.Copy).then_inc(out_ready, 1)

        @block.vector
        def _(dve):
            at = Place()
            step = Tally()
            add, mult, sub = ALU.add, ALU.mult, ALU.subtract

            def mark(ins):
                ins.then_inc(dve_step, 1)
                return step.next()

            def after_all():
                dve.wait_ge(dve_step, step.now())

            def settle():
                after_all()
                if at.operand.n:
                    dve.wait_ge(op_lo, at.operand.now())

            def look(kind="plain"):
                split_lo(dve, 1, at, kind)

            def enter(j, mixed, nxt=None):
                for _ in range(2 if mixed and j % GROUP == GROUP - 1 else 1):
                    look(next(nxt) if nxt else "plain")

            def leave(j, mixed, nxt=None):
                if mixed and j % GROUP < GROUP - 1:
                    look(next(nxt) if nxt else "plain")

            def full():
                t = at.tile()
                dve.wait_ge(tile_done, t.done)
                return t

            def through(t):
                dve.wait_ge(drained[t.bank], t.drained)

            def mod_add(l, first):
                dve.wait_ge(mod_cols, at.group.next())
                for s in range(2):
                    last = dve.tensor_tensor(
                        MOD[:, l, bass.ds(first, GROUP), s],
                        PT[:, 0:2 * GROUP].rearrange("p (f s) -> p f s", s=2)[:, :, s],
                        PAR[:, 2, bass.ds(first + l * NMOD * DT, GROUP)], add)
                last.then_inc(mod_done, 1)

            def take_root(n, roots):
                t = at.tile()
                settle()
                dve.wait_ge(root_done, roots)
                dve.reciprocal(RSTD[:, 0:n], ROOT[:, 0:n]).then_inc(drained[t.bank], 1)
                through(t)

            def low(dst, src, hi, scale=None, shift=None):
                dve.wait_ge(op_hi, at.operand.now() + 1)
                if scale is not None:
                    ins = [dve.scalar_tensor_tensor(dst, src, scale, hi.bitcast(F32), mult, sub)]
                elif shift is not None:
                    ins = [dve.scalar_tensor_tensor(dst[:, h], src[:, h], b, hi[:, h].bitcast(F32), add, sub)
                           for h, b in shift]
                else:
                    ins = [dve.tensor_tensor(dst, src, hi.bitcast(F32), sub)]
                ins[-1].then_inc(op_lo, 1)
                at.operand.next()

            def normed_h(l, mod, gain, n_streams):
                settle()
                for s in range(n_streams):
                    mark(dve.scalar_tensor_tensor(AV[:, :, s], MOD[:, l, (mod + 1) * DT:(mod + 2) * DT, s], 1.0,
                                                  PAR[:, l, gain:gain + DT], add, mult))
                after_all()

                def low_part(k):
                    low(Hlo[:, k, :], Z[:, k % 2, :], Hhi[:, k, :],
                        shift=[(half[s], MOD[:, l, mod * DT + k, s:s + 1]) for s in range(n_streams)])

                for k in range(DT):
                    settle()
                    for s in range(n_streams):
                        last = dve.scalar_tensor_tensor(Z[:, k % 2, half[s]], X[:, k, half[s]], AV[:, k, s:s + 1],
                                                        RSTD[:, half[s]], mult, mult)
                    last.then_inc(z_done, 1)
                    if k:
                        low_part(k - 1)
                low_part(DT - 1)

            def normed(l, n, tiles, raw0, to, gain):
                def low_part(k):
                    low(Ulo[:, to + k, 0:n], Z[:, k % 2, 0:n], Uhi[:, to + k, 0:n])

                for k in range(tiles):
                    settle()
                    dve.scalar_tensor_tensor(Z[:, k % 2, 0:n], G[:, raw0 + k, 0:n],
                                             PAR[:, l, gain + k:gain + k + 1], RSTD[:, 0:n],
                                             mult, mult).then_inc(z_done, 1)
                    if k:
                        low_part(k - 1)
                low_part(tiles - 1)

            def keep_raw(k, n):
                t = full()
                dve.wait_ge(sq_done, at.square.next())
                dve.tensor_copy(G[:, k, 0:n], banks[t.bank][:, 0:n]).then_inc(drained[t.bank], 1)

            t = full()
            dve.tensor_copy(PAR[:, 3, 0:CVEC + 2 * DT], banks[t.bank][:, 0:CVEC + 2 * DT]).then_inc(
                drained[t.bank], 1)
            dve.wait_ge(cond_tanh, 1)
            CSf = CS[:, :, :].rearrange("p s k -> p (s k)")
            mark(dve.scalar_tensor_tensor(CSf, CTH[:, :], 1.0, PAR[:, 3, CVEC:CVEC + 2 * DT], add, mult))
            after_all()
            cv = [CV[:, :, 2 * j:2 * j + 2].rearrange("p k s -> p s k") for j in range(2)]
            mark(dve.tensor_scalar(cv[0], CS[:, :, :], 0.5, None, mult))
            after_all()
            dve.scalar_tensor_tensor(cv[1], CS[:, :, :], 0.5, cv[0].bitcast(F32), mult, sub).then_inc(cond_done, 1)
            for _ in range(AHEAD):
                look()
            for g in range(4):
                for q in range(GROUP):
                    if q == 2 and g:
                        mod_add(0, (g - 1) * GROUP)
                    if g in (1, 2):
                        t = full()
                        dve.tensor_copy(X[:, (g - 1) * GROUP + q, :], banks[t.bank][:, :]).then_inc(
                            drained[t.bank], 1)
                        at.square.next()
                    look()
                if g == 0:
                    t = full()
                    for b, n in enumerate((ROWS, ROWS, 2 * NMOD * DT)):
                        last = dve.tensor_copy(PAR[:, b, 0:n], banks[t.bank][:, b * P:b * P + n])
                    last.then_inc(drained[t.bank], 1)
                    through(t)
            at.split_by_slot = True
            take_root(T, stat_root(0, 0))
            mod_add(0, 3 * GROUP)
            dve.wait_ge(padded, 2)
            for l in range(DEPTH):
                TQ = NS[l] * SEQ
                dve.wait_ge(mod_done, at.group.n)
                normed_h(l, 0, LN1, 2)
                nxt = ahead(projection_kinds(l), PAIR_KINDS)
                tile_no = 0

                def step_in():
                    enter(tile_no, l == 0, nxt)

                def step_out():
                    nonlocal tile_no
                    leave(tile_no, l == 0, nxt)
                    tile_no += 1
                    if l == 0 and tile_no % GROUP == 0:
                        mod_add(0, 16 + tile_no - GROUP)

                for j in range(2):
                    step_in()
                    keep_raw(j, T)
                    step_out()
                step_in()
                tanh_g = [at.tile()]
                step_out()
                step_in()
                settle()
                t = full()
                mark(dve.tensor_tensor(Z[64:96, 0, :], banks[t.bank][0:32, :], TAB[0:32, :], mult))
                dve.tensor_tensor(Z[64:96, 1, :], banks[t.bank][32:64, :], TAB[32:64, :], mult).then_inc(
                    drained[t.bank], 1)
                after_all()
                through(t)
                for h in range(2):
                    mark(dve.tensor_tensor(Kb[64:96, h, :], Z[64:96, 0, :], Z[64:96, 1, :], add))
                step_out()
                step_in()
                take_root(T, stat_root(l, 1))
                normed(l, T, 2, 0, CT0, KVG)
                for j in range(3):
                    if j:
                        step_in()
                    keep_raw(2 + j, TQ)
                    step_out()
                step_in()
                tanh_g.append(at.tile())
                step_out()
                take_root(TQ, stat_root(l, 2))
                normed(l, TQ, 3, 2, QT, QG)
                for j in range(2):
                    step_in()
                    t = full()
                    dve.wait_ge(drained[tanh_g[j].bank], tanh_g[j].drained)
                    dve.scalar_tensor_tensor(U[:, j, 0:NS[l], PAD:PAD + SEQ], by_stream(TG[:, j, :], l), 1.0,
                                             by_stream(banks[t.bank][:, :], l), add, mult).then_inc(
                                                 drained[t.bank], 1)
                    step_out()
                through(t)

                def tap(w, start):
                    for j in range(2):
                        dve.wait_ge(dve_step, step.now() - 1)
                        mark(dve.scalar_tensor_tensor(
                            by_stream(ACC[:, j, :], l), U[:, j, 0:NS[l], bass.ds(start, SEQ)],
                            PAR[:, l, bass.ds(w + j, 1)], by_stream(ACC[:, j, :], l), mult, add))

                for j in range(2):
                    mark(dve.tensor_scalar(by_stream(ACC[:, j, :], l), U[:, j, 0:NS[l], 0:SEQ],
                                           PAR[:, l, CDW + j:CDW + j + 1], None, mult))
                gates = []
                for j in range(2):
                    step_in()
                    gates.append(at.tile())
                    tap(CDW + 2 * (j + 1), j + 1)
                    step_out()
                for j in range(2):
                    step_in()
                    t = full()
                    dve.wait_ge(drained[gates[j].bank], gates[j].drained)
                    dve.tensor_tensor(C[:, j, 0:NS[l], 1:1 + SEQ], by_stream(TG[:, j, :], l),
                                      by_stream(banks[t.bank][:, :], l), mult).then_inc(drained[t.bank], 1)
                    step_out()
                through(t)
                for w in range(SC_TAPS):
                    for j in range(2):
                        wt = PAR[:, l, SCW + 2 * w + j:SCW + 2 * w + j + 1]
                        src, acc = C[:, j, 0:NS[l], w:w + SEQ], by_stream(Z[:, j, :], l)
                        if w == 0:
                            mark(dve.tensor_scalar(acc, src, wt, None, mult))
                        else:
                            dve.wait_ge(dve_step, step.now() - 1)
                            mark(dve.scalar_tensor_tensor(acc, src, wt, acc, mult, add))
                for j in range(2):
                    step_in()
                    t = at.tile()
                    dve.wait_ge(drained[t.bank], t.drained)
                    dve.wait_ge(dve_step, step.now() - 1 + j)
                    mark(dve.tensor_tensor(BG[:, j, 0:TQ], BG[:, j, 0:TQ], Z[:, j, 0:TQ], mult))
                    step_out()

                units = units_of(l)

                def pair(p, after):
                    nxt = ahead(PAIR_KINDS, after)
                    taps = iter(range(TAPS_BEFORE, TAPS_BEFORE + TAPS_PER_PAIR))

                    def do_taps(n):
                        for w in [next(taps) for _ in range(n)]:
                            tap(p * (2 * TAPS_PER_PAIR) + (CDW + 2 * w), p * TAPS_PER_PAIR + w)

                    do_taps(1)
                    look(next(nxt))
                    look(next(nxt))
                    do_taps(1)
                    at.tile()
                    at.tile()
                    after_all()
                    for h in range(2):
                        t = full()
                        bank = banks[t.bank]
                        if h:
                            dve.wait_ge(q_ready, at.heads.now())
                        mark(dve.scalar_tensor_tensor(Z[64:96, 0, 0:TQ], bank[64:96, 0:TQ], SCALE,
                                                      TAB[64:96, 0:TQ], mult, mult))
                        dve.wait_ge(q_nope, at.heads.next())
                        dve.scalar_tensor_tensor(Z[64:96, 1, 0:TQ], bank[96:128, 0:TQ], SCALE,
                                                 TAB[96:128, 0:TQ], mult, mult).then_inc(drained[t.bank], 1)
                        after_all()
                        through(t)
                        dve.tensor_tensor(Qb[64:96, h, 0:TQ], Z[64:96, 0, 0:TQ], Z[64:96, 1, 0:TQ],
                                          add).then_inc(q_ready, 1)
                    base = at.unit.n

                    def unit(k):
                        return at.unit.now() - (at.unit.n - base) + k

                    def row_max(u):
                        kt = units[u][3]
                        dve.wait_ge(qk_done, unit(u + 1))
                        dve.tensor_reduce(NM[:, u % 2:u % 2 + 1], S[u % 2][:, 0:kt * P], AX.X, ALU.max,
                                          negate=True).then_inc(max_done, 1)

                    def normalise(u):
                        kt = units[u][3]
                        dve.wait_ge(exp_done, unit(u + 1))
                        mark(dve.reciprocal(RR[:, u % 2:u % 2 + 1], RS[:, u % 2:u % 2 + 1]))
                        after_all()
                        dve.tensor_scalar(PR[:, u % 2, 0:kt * P], PR[:, u % 2, 0:kt * P],
                                          RR[:, u % 2:u % 2 + 1], None, mult).then_inc(prob_done, 1)

                    row_max(0)
                    row_max(1)
                    normalise(0)
                    normalise(1)
                    look(next(nxt))
                    look(next(nxt))
                    do_taps(1)
                    for u in range(2, len(units)):
                        row_max(u)
                        normalise(u)
                    do_taps(TAPS_PER_PAIR - 3)
                    for _ in units:
                        at.unit.next()
                    at.tile()
                    at.tile()
                    low(Ulo[:, p + AT0, 0:TQ], PV[:, 0:TQ], Uhi[:, p + AT0, 0:TQ])

                steps = 2 + 2 * TAPS_PER_PAIR + len(units)
                with at.loop(dve, PAIRS - 1, chunks=4, tiles=6, units=len(units), operands=1, heads=2,
                             extra=[(step, steps)]) as i:
                    pair(i, PAIR_KINDS)
                pair(PAIRS - 1, ["plain"] * AHEAD)

                nxt = ahead(["plain"] * 4, branch_kinds(l))

                def attended(m):
                    t = full()
                    dve.scalar_tensor_tensor(G[:, m, 0:TQ], G[:, m, 0:TQ], 1.0, banks[t.bank][:, 0:TQ],
                                             add, mult).then_inc(drained[t.bank], 1)

                look(next(nxt))
                after_all()
                for j in range(2):
                    last = dve.tensor_scalar(ACC[:, j, 0:TQ], ACC[:, j, 0:TQ], 0.5,
                                             PAR[:, l, CB + j:CB + j + 1], mult, add)
                last.then_inc(conv_a, 1)
                for j in range(2):
                    low(Ulo[:, SO0 + j, 0:TQ], BG[:, j, 0:TQ], Uhi[:, SO0 + j, 0:TQ])
                attended(0)
                attended(1)
                look(next(nxt))
                t = full()
                dve.wait_ge(conv_a, l + 1)
                for j in range(2):
                    last = dve.scalar_tensor_tensor(ACC[:, j, 0:TQ], banks[t.bank][:, 0:TQ], -1.0 / CH,
                                                    ACC[:, j, 0:TQ], mult, add)
                last.then_inc(drained[t.bank], 1)
                attended(2)
                attended(3)
                look(next(nxt))
                take_root(TQ, stat_root(l, 3))
                for j in range(2):
                    mark(dve.tensor_tensor(Z[:, j, 0:TQ], ACC[:, j, 0:TQ], RSTD[:, 0:TQ], mult))
                after_all()
                for j in range(2):
                    last = dve.tensor_scalar(ACC[:, j, 0:TQ], Z[:, j, 0:TQ], PAR[:, l, LNG + j:LNG + j + 1],
                                             PAR[:, l, LNB + j:LNB + j + 1], mult, add)
                last.then_inc(conv_v, 1)
                dve.wait_ge(conv_t, l + 1)
                dve.wait_ge(conv_v, l + 1)
                for j in range(2):
                    last = dve.scalar_tensor_tensor(Z[:, j, 0:TQ], TG[:, j, 0:TQ], 1.0, ACC[:, j, 0:TQ], add, mult)
                last.then_inc(conv_s, 1)
                for j in range(2):
                    low(Ulo[:, CO0 + j, 0:TQ], Z[:, j, 0:TQ], Uhi[:, CO0 + j, 0:TQ], scale=0.5)
                for m in range(4, DT):
                    if m == 6:
                        look(next(nxt))
                    attended(m)

                settle()

                def branches(i, after):
                    nxt = ahead(branch_kinds(l), after)
                    free = [(2 + j, at.uses[2 + j].now()) for j in range(2)]
                    for m in range(2):
                        gates = []
                        for j in range(2):
                            enter(2 * m + j, l == 0, nxt)
                            gates.append(at.tile())
                            leave(2 * m + j, l == 0, nxt)
                        for j in range(2):
                            look(next(nxt))
                            t = full()
                            dve.wait_ge(drained[gates[j].bank], gates[j].drained)
                            dve.wait_ge(drained[free[j][0]], free[j][1])
                            mark(dve.scalar_tensor_tensor(Z[:, j, 0:TQ], TG[:, j, 0:TQ], 1.0,
                                                          banks[t.bank][:, 0:TQ], add, mult))
                            after_all()
                            if j:
                                through(t0)
                            dve.tensor_tensor(G[:, i * 2 + m, 0:TQ], G[:, i * 2 + m, 0:TQ], Z[:, j, 0:TQ],
                                              add).then_inc(drained[t.bank], 1)
                            free[j], t0 = (t.bank, t.drained), t
                    if l == 0:
                        mod_add(0, i * GROUP + 32)

                with at.loop(dve, 3, chunks=12 if l == 0 else 8, tiles=8, groups=1 if l == 0 else 0,
                             extra=[(step, 4)]) as i:
                    branches(i, branch_kinds(l))
                at.ring = 0
                branches(3, ["plain"] * AHEAD)
                for k in range(DT):
                    low(Hlo[:, k, 0:TQ], G[:, k, 0:TQ], Hhi[:, k, 0:TQ], scale=0.5)

                def residual(m, mod):
                    t = full()
                    for s in range(NS[l]):
                        last = dve.scalar_tensor_tensor(X[:, m, half[s]], banks[t.bank][:, half[s]],
                                                        MOD[:, l, m + mod * DT, s:s + 1], X[:, m, half[s]],
                                                        mult, add)
                    last.then_inc(drained[t.bank], 1)
                    return t

                for j in range(DT):
                    mixed = l == 0 and j >= GROUP
                    enter(j, mixed)
                    residual(j, 2)
                    leave(j, mixed)
                if l == 0:
                    mod_add(1, 0)
                at.square.n += DT
                take_root(TQ, stat_root(l, 4))
                normed_h(l, 3, LN2, NS[l])
                first = 0
                for g, n in enumerate(FF_GROUPS):
                    mixed = 1 if l == 0 else 0
                    with at.loop(dve, n // 2, chunks=4 + 4 * mixed, tiles=4, operands=2, gates=2, groups=mixed) as i:
                        free = [at.uses[2 + j].now() for j in range(2)]
                        for j in range(2):
                            enter(j, mixed)
                            t = full()
                            dve.wait_ge(gate_tanh, at.gates.next())
                            dve.wait_ge(drained[2 + j], free[j])
                            dve.scalar_tensor_tensor(Z[:, j, 0:TQ], TG[:, j, 0:TQ], 1.0, banks[t.bank][:, 0:TQ],
                                                     add, mult).then_inc(drained[t.bank], 1)
                            leave(j, mixed)
                        through(t)
                        dve.wait_ge(op_lo, at.operand.now())
                        for j in range(2):
                            enter(2 + j, mixed)
                            t = full()
                            dve.scalar_tensor_tensor(PR[:, j, 0:TQ], Z[:, j, 0:TQ], 0.5, banks[t.bank][:, 0:TQ],
                                                     mult, mult).then_inc(drained[t.bank], 1)
                            low(Ulo[:, i * 2 + j, 0:TQ], PR[:, j, 0:TQ], Uhi[:, i * 2 + j, 0:TQ])
                            leave(2 + j, mixed)
                        if mixed:
                            mod_add(1, i * GROUP + (GROUP + 2 * first))
                    first += n
                    if g == len(FF_GROUPS) - 1 and l == DEPTH - 1:
                        for j in range(8):
                            if j < DT - AHEAD:
                                look()
                            residual(j, 5)
                    else:
                        with at.loop(dve, 2, chunks=4, tiles=4) as i:
                            for j in range(4):
                                look()
                                residual(i * 4 + j, 5)
                at.square.n += DT
                take_root(T if l == 0 else SEQ, stat_root(l + 1, 0))
            for k in range(DT):
                dve.scalar_tensor_tensor(G[:, k, 0:SEQ], X[:, k, 0:SEQ], PAR[:, 3, FING + k:FING + k + 1],
                                         RSTD[:, 0:SEQ], mult, mult).then_inc(fin_z, 1)

        @block.tensor
        def _(pe):
            at = Place()

            def new_tile():
                t = at.tile()
                if not isinstance(t.before, int) or t.before > 0:
                    pe.wait_ge(drained[t.bank], t.before)
                return t

            def chunk():
                slot, n = at.chunk.n % SLOTS, at.chunk.n
                if at.chunk.var is None:
                    pe.wait_ge(lo_done[slot], n // SLOTS + 1)
                else:
                    pe.wait_ge(lo_done[slot], at.chunk.var * (at.chunk.step // SLOTS) + (n // SLOTS + 1))
                at.chunk.next()
                return slot

            def split_product(dst, k, terms, ready=None):
                for j in range(k):
                    if ready is not None:
                        pe.wait_ge(op_lo, ready + j + 1)
                    sh, sl, mh, ml = terms(j)
                    pe.matmul(dst, sh, mh, start=j == 0, stop=False)
                    pe.matmul(dst, sh, ml, start=False, stop=False)
                    last = pe.matmul(dst, sl, mh, start=False, stop=j == k - 1)
                return last

            def gemm(slot, width, col, m, k, ops, o0, n, ready=None):
                t = new_tile()
                oh, ol = ops

                def terms(j):
                    a = j * width + col
                    return (Whi[:, slot, a:a + m], Wlo[:, slot, a:a + m],
                            oh[:, o0 + j, 0:n], ol[:, o0 + j, 0:n])

                last = split_product(banks[t.bank][0:m, 0:n], k, terms, ready)
                return t, last

            H, O = (Hhi, Hlo), (Uhi, Ulo)

            def tile_of(m, k, ops, o0, n, ready=None, width=None):
                _, last = gemm(chunk(), width or m, 0, m, k, ops, o0, n, ready)
                last.then_inc(tile_done, 1)

            def tiles_together(slots, ns, ready):
                tiles = [new_tile() for _ in slots]
                for j in range(DT):
                    pe.wait_ge(op_lo, ready + j + 1)
                    for t, slot, n in zip(tiles, slots, ns):
                        w, dst = slice(j * P, (j + 1) * P), banks[t.bank][:, 0:n]
                        pe.matmul(dst, Whi[:, slot, w], Hhi[:, j, 0:n], start=j == 0, stop=False)
                        pe.matmul(dst, Whi[:, slot, w], Hlo[:, j, 0:n], start=False, stop=False)
                        last = pe.matmul(dst, Wlo[:, slot, w], Hhi[:, j, 0:n], start=False, stop=j == DT - 1)
                        if j == DT - 1:
                            last.then_inc(tile_done, 1)

            def first_tiles(mixed, ns, ready):
                slots = [chunk()]
                if mixed:
                    mod_chunk(0)
                slots.append(chunk())
                if not mixed:
                    slots.append(chunk())
                tiles_together(slots, ns, ready)
                if mixed:
                    mod_chunk(1)
                return len(slots)

            def mixed_tile(j, mixed, tile):
                if mixed and j % GROUP == GROUP - 1:
                    mod_chunk(j % GROUP)
                tile()
                if mixed and j % GROUP < GROUP - 1:
                    mod_chunk(j % GROUP)

            def total(n):
                pe.wait_ge(sq_summed, at.square.now())
                t = new_tile()
                pe.matmul(banks[t.bank][:, 0:n], ONES[:, :], SUM[:, 0:n], start=True, stop=True).then_inc(tile_done, 1)

            def mod_chunk(q, bank=0):
                slot = chunk()
                if q == 0 and at.group.n:
                    pe.wait_ge(mod_rows, at.group.now())
                for k in range(DT):
                    for w in (Whi, Wlo):
                        last = pe.matmul(S[bank][0:4, q * CW:(q + 1) * CW], CV[:, k, :], w[:, slot, k * CW:(k + 1) * CW],
                                         start=k == 0 and w is Whi, stop=k == DT - 1 and w is Wlo)
                last.then_inc(mod_used, 1)

            def mod_turn():
                if at.group.n:
                    pe.wait_ge(mod_done, at.group.now())
                pe.wait_ge(mod_rows, at.group.next())
                for f in range(GROUP):
                    last = pe.matmul(PT[:, 2 * f:2 * f + 2], ROW[:, f * P:(f + 1) * P], SEL[:, :],
                                     start=True, stop=True)
                last.then_inc(mod_cols, 1)

            pe.wait_ge(consts, 3)
            pe.wait_ge(shared_in, 48)
            t = new_tile()
            n = CVEC + 2 * DT
            pe.transpose(banks[t.bank][:, 0:n], PST[0:n, 0, 3 * P:4 * P], IDN[0:n, 0:n]).then_inc(tile_done, 1)
            pe.wait_ge(cond_done, 1)
            for g in range(4):
                for q in range(GROUP):
                    mod_chunk(q, g % 2)
                    if q == 1 and g:
                        mod_turn()
                    if g in (1, 2):
                        if g == 1 and q == 0:
                            pe.wait_ge(x_in, 32)
                        k = (g - 1) * GROUP + q
                        t = new_tile()
                        for j in range(4):
                            src = G[:, 2 * j + k // 4, (k % 4) * P:(k % 4 + 1) * P]
                            last = pe.transpose(banks[t.bank][:, j * P:(j + 1) * P], src, IDN[:, :])
                        last.then_inc(tile_done, 1)
                        at.square.next()
                if g == 0:
                    pe.wait_ge(vec_in, 16 * N_VEC)
                    t = new_tile()
                    for b, n in enumerate((ROWS, ROWS, 2 * NMOD * DT)):
                        last = pe.transpose(banks[t.bank][:, b * P:b * P + n], PST[0:n, 0, b * P:(b + 1) * P],
                                            IDN[0:n, 0:n])
                    last.then_inc(tile_done, 1)
            total(T)
            mod_turn()
            for l in range(DEPTH):
                TQ = NS[l] * SEQ
                o = at.operand.n
                tile_no = first_tiles(l == 0, (T, T, TQ), o)
                at.square.n += 2

                def projection(n, m=P):
                    nonlocal tile_no
                    mixed_tile(tile_no, l == 0, lambda: tile_of(m, DT, H, 0, n, o))
                    tile_no += 1
                    if l == 0 and tile_no % GROUP == 0:
                        mod_turn()

                if tile_no < AHEAD:
                    projection(TQ)
                projection(T, 2 * ROPE)
                total(T)
                for _ in range(3):
                    projection(TQ)
                at.square.n += 3
                projection(TQ)
                total(TQ)
                for _ in range(8):
                    projection(TQ)
                at.operand.n += DT + 5

                units = units_of(l)

                def gate_tile(halfway=None):
                    slot, t = chunk(), new_tile()
                    for j in range(DT):
                        if j == DT // 2 and halfway:
                            halfway()
                        w, dst = slice(j * P, (j + 1) * P), banks[t.bank][:, 0:TQ]
                        pe.matmul(dst, Whi[:, slot, w], Hhi[:, j, 0:TQ], start=j == 0, stop=False)
                        pe.matmul(dst, Whi[:, slot, w], Hlo[:, j, 0:TQ], start=False, stop=False)
                        last = pe.matmul(dst, Wlo[:, slot, w], Hhi[:, j, 0:TQ], start=False, stop=j == DT - 1)
                    last.then_inc(tile_done, 1)

                def pair(first):
                    slot = chunk()
                    wkv = [w[:, slot, 0:4 * P].rearrange("p (k e n) -> p k e n", k=2, e=2) for w in (Whi, Wlo)]
                    keys = new_tile()
                    split_product(banks[keys.bank][:, :], 2,
                                  lambda k: (wkv[0][:, k, 0, :], wkv[1][:, k, 0, :],
                                             Uhi[:, CT0 + k, :], Ulo[:, CT0 + k, :])).then_inc(tile_done, 1)
                    values = new_tile()
                    for tt in range(4):
                        cols = slice(tt * P, (tt + 1) * P)
                        last = split_product(banks[values.bank][:, cols], 2,
                                             lambda k: (Uhi[:, CT0 + k, cols], Ulo[:, CT0 + k, cols],
                                                        wkv[0][:, k, 1, :], wkv[1][:, k, 1, :]))
                    last.then_inc(tile_done, 1)
                    slot = chunk()
                    wq = [w[:, slot, 0:6 * P].rearrange("p (g n) -> p g n", g=6) for w in (Whi, Wlo)]
                    for h in range(2):
                        t = new_tile()
                        split_product(banks[t.bank][:, 0:TQ], 3,
                                      lambda k: (wq[0][:, 2 * k + h, :], wq[1][:, 2 * k + h, :],
                                                 Uhi[:, QT + k, 0:TQ], Ulo[:, QT + k, 0:TQ])).then_inc(tile_done, 1)
                    base = at.unit.n

                    def unit(k):
                        return at.unit.now() - (at.unit.n - base) + k

                    pe.wait_ge(drained[keys.bank], keys.drained)
                    pe.wait_ge(drained[values.bank], values.drained)
                    q0 = at.heads.now()

                    def scores(u):
                        h, col, k0, kt = units[u]
                        pe.wait_ge(q_ready, q0 + h + 1)
                        if u >= 2:
                            pe.wait_ge(exp_done, unit(u - 1))
                        pe.matmul(S[u % 2][:, 0:kt * P], Qb[:, h, col:col + P], Kb[:, h, k0 * P:(k0 + kt) * P],
                                  start=True, stop=True).then_inc(qk_done, 1)

                    def turn(u):
                        kt = units[u][3]
                        pe.wait_ge(prob_done, unit(u + 1))
                        if u:
                            pe.wait_ge(turned_copied, unit(u))
                        for k in range(kt):
                            last = pe.transpose(PT[:, k * P:(k + 1) * P], PR[:, u % 2, k * P:(k + 1) * P], IDN[:, :])
                        last.then_inc(turned, 1)

                    def values_of(u):
                        h, col, k0, kt = units[u]
                        if u == 0:
                            pe.wait_ge(op_lo, at.operand.now())
                        pe.wait_ge(turned_copied, unit(u + 1))
                        for k in range(kt):
                            last = pe.matmul(PV[h * VH:(h + 1) * VH, col:col + P], V[:, k0 + k, h * VH:(h + 1) * VH],
                                             PTs[:, u % 2, k * P:(k + 1) * P], start=k == 0, stop=k == kt - 1)
                        last.then_inc(pv_done, 1)

                    n = len(units)
                    scores(0)
                    scores(1)
                    gate_tile()
                    for u in range(2, n):
                        scores(u)
                        turn(u - 2)
                        if u > 2:
                            values_of(u - 3)
                    turn(n - 2)
                    values_of(n - 3)

                    def last_turn():
                        turn(n - 1)
                        values_of(n - 2)

                    gate_tile(last_turn)
                    values_of(n - 1)
                    for _ in units:
                        at.unit.next()
                    at.heads.next()
                    at.heads.next()
                    at.operand.next()

                pe.wait_ge(op_lo, at.operand.n)
                with at.loop(pe, PAIRS - 1, chunks=4, tiles=6, units=len(units), operands=1, heads=2) as i:
                    pair(i)
                pair(None)

                pe.wait_ge(op_lo, at.operand.n)
                def mla():
                    slot = chunk()
                    for q in range(2):
                        _, last = gemm(slot, 2 * CW, q * P, P, 4, O, AT0, TQ)
                        last.then_inc(tile_done, 1)

                def over_channels(src):
                    t = new_tile()
                    for j in range(2):
                        last = pe.matmul(banks[t.bank][:, 0:TQ], ONES[:, :], src[:, j, 0:TQ], start=j == 0, stop=j == 1)
                    last.then_inc(tile_done, 1)

                mla()
                pe.wait_ge(conv_a, l + 1)
                over_channels(ACC)
                mla()
                pe.wait_ge(conv_sq, l + 1)
                over_channels(SQ)
                mla()
                mla()
                at.operand.n += 4

                with at.loop(pe, 4, chunks=12 if l == 0 else 8, tiles=8, groups=1 if l == 0 else 0):
                    for m in range(2):
                        for j in range(2):
                            mixed_tile(2 * m + j, l == 0, lambda: tile_of(P, DT, H, 0, TQ))
                        pe.wait_ge(op_lo, at.operand.n)
                        for o0 in (CO0, SO0):
                            tile_of(P, 2, O, o0, TQ)
                    if l == 0:
                        mod_turn()
                o = at.operand.n
                at.operand.n += DT
                for j in range(first_tiles(False, (TQ,) * AHEAD, o), DT):
                    mixed_tile(j, l == 0 and j >= GROUP, lambda: tile_of(P, DT, H, 0, TQ, o))
                if l == 0:
                    mod_turn()
                at.square.n += DT
                total(TQ)
                o = at.operand.n
                at.operand.n += DT
                for g, n in enumerate(FF_GROUPS):
                    mixed = 1 if l == 0 else 0

                    def hidden(done):
                        for j in range(done, 4):
                            mixed_tile(j, mixed, lambda: tile_of(P, DT, H, 0, TQ, o))
                        at.operand.next()
                        at.operand.next()
                        if mixed:
                            mod_turn()

                    if g == 0:
                        at.ring = 0
                        hidden(first_tiles(mixed, (TQ,) * AHEAD, o))
                    with at.loop(pe, n // 2 - (1 if g == 0 else 0), chunks=4 + 4 * mixed, tiles=4,
                                 operands=2, groups=mixed):
                        hidden(0)
                    up = at.operand.n - n
                    if g == len(FF_GROUPS) - 1 and l == DEPTH - 1:
                        for j in range(8):
                            tile_of(P, n, O, 0, TQ, up)
                    else:
                        with at.loop(pe, 2, chunks=4, tiles=4):
                            for j in range(4):
                                tile_of(P, n, O, 0, TQ, up)
                at.square.n += DT
                total(SEQ if l == DEPTH - 1 else T)
            for h in range(2):
                tiles = [new_tile() for _ in range(2)]
                for k in range(4):
                    pe.wait_ge(fin_z, 4 * h + k + 1)
                    for j, t in enumerate(tiles):
                        last = pe.transpose(banks[t.bank][:, k * P:(k + 1) * P],
                                            G[:, 4 * h + k, j * P:(j + 1) * P], IDN[:, :])
                        if k == 3:
                            last.then_inc(tile_done, 1)


_INS = ["x", "c", "ctx", "c_ctx", "w_mod", "b_mod", "ln1_g", "w_in", "q_a_norm_g", "w_q_b", "kv_a_norm_g",
        "w_kv_b", "w_mla_o", "conv_dw", "conv_dw_b", "conv_ln_g", "conv_ln_b", "w_conv_o", "sc_dw", "w_sc_o",
        "w_o", "ln2_g", "w_ff1", "w_ff3", "w_ff2", "final_g"]


def kernel(**inputs):
    import numpy as np
    import concourse.bacc as bacc
    from concourse.bass_utils import run_bass_kernel_spmd

    nc = bacc.Bacc("TRN2", target_bir_lowering=False, num_devices=1)
    arrays, args = {}, []
    for name in _INS:
        a = np.ascontiguousarray(inputs[name])
        arrays[f"in_{name}"] = a
        args.append(nc.dram_tensor(f"in_{name}", a.shape, mybir.dt.from_np(a.dtype), kind="ExternalInput").ap())
    token = np.arange(SEQ)
    inv = np.power(np.float32(10000.0), -np.arange(0, ROPE // 2, 2, dtype=np.float32) / np.float32(ROPE // 2))
    cos, sin = np.ones((ROPE, T), np.float32), np.zeros((ROPE, T), np.float32)
    for r in range(ROPE):
        pos = (token // GRID_W if r < ROPE // 2 else token % GRID_W).astype(np.float32)
        angle = pos * inv[r % 8]
        cos[r, :SEQ] = np.cos(angle)
        sin[r, :SEQ] = np.sin(angle) * (-1 if r % 16 < 8 else 1)
    arrays["rope"] = np.concatenate([cos, sin, cos, sin])
    args.append(nc.dram_tensor("rope", (P, T), mybir.dt.float32, kind="ExternalInput").ap())
    args.append(nc.dram_tensor("out", (1, SEQ, D), mybir.dt.float32, kind="ExternalOutput").ap())
    build(nc, *args)
    r = run_bass_kernel_spmd(nc, [arrays], core_ids=[0])
    return r.results[0]["out"]
```
